# Optimizing a Trainium2 kernel written in Bass

```python
import math
import jax, jax.numpy as jnp
from jax import lax
import numpy as np

D_MODEL = 1024
BATCH = 1
SEQ = 256
DEPTH = 4

N_MIXERS = 3
N_A = (DEPTH + 2) // 3
N_B = (DEPTH + 1) // 3
N_C = DEPTH // 3
BLOCK = 128
N_META = 16
PAD = BLOCK - N_META
NEG = -1e30

DEEPNORM_ALPHA = (2.0 * DEPTH) ** 0.25
DEEPNORM_BETA = (8.0 * DEPTH) ** -0.25
LN_EPS = 1e-5
RMS_EPS = 1e-6

FOX_HEADS = 16
FOX_HEAD_DIM = 64
FOX_GATE_BIAS = 4.0

SWA_Q_HEADS = 16
SWA_KV_HEADS = 2
SWA_HEAD_DIM = 64
WINDOW = 128
ROPE_THETA = 500000.0
ROPE_DIM = SWA_HEAD_DIM // 4

MLA_HEADS = 16
MLA_Q_LORA = 384
MLA_KV_LORA = 256
MLA_NOPE = 64
MLA_ROPE = 32
MLA_V = 64
MLA_ROPE_THETA = 10000.0

D_FF = 2816
CONV_W = 3

kernel_name = "hybrid_fox_swa_mla_convffn_trunk"

def layer_norm(x, g, b):
    xf = x.astype(jnp.float32)
    mu = jnp.mean(xf, axis=-1, keepdims=True)
    var = jnp.mean(jnp.square(xf - mu), axis=-1, keepdims=True)
    return ((xf - mu) * lax.rsqrt(var + LN_EPS) * g + b).astype(x.dtype)

def rms_norm(x, g):
    xf = x.astype(jnp.float32)
    return (xf * lax.rsqrt(jnp.mean(jnp.square(xf), axis=-1, keepdims=True) + RMS_EPS) * g).astype(x.dtype)

def rope_angles(pos, dim, theta):
    inv = theta ** (-jnp.arange(0, dim, 2, dtype=jnp.float32) / dim)
    ang = pos.astype(jnp.float32)[:, None] * inv[None, :]
    return jnp.cos(ang), jnp.sin(ang)

def apply_rope(x, cos, sin):
    x1, x2 = jnp.split(x.astype(jnp.float32), 2, axis=-1)
    c = cos[None, :, None, :]
    s = sin[None, :, None, :]
    return jnp.concatenate([x1 * c - x2 * s, x1 * s + x2 * c], axis=-1).astype(x.dtype)

def partial_rope(x, cos, sin):
    return jnp.concatenate([apply_rope(x[..., :ROPE_DIM], cos, sin), x[..., ROPE_DIM:]], axis=-1)

def dense_causal_attention(q, k, v, decay=None):
    B, L, H, dk = q.shape
    nblk = L // BLOCK
    scale = dk ** -0.5
    kpos = jnp.arange(L)
    kvalid = kpos >= PAD
    qb = q.reshape(B, nblk, BLOCK, H, dk).transpose(1, 0, 2, 3, 4)
    xs = (jnp.arange(nblk), qb)
    if decay is not None:
        ck = decay.transpose(0, 2, 1)
        cb = decay.reshape(B, nblk, BLOCK, H).transpose(1, 0, 3, 2)
        xs = xs + (cb,)

    def one_block(args):
        i, qi = args[0], args[1]
        s = jnp.einsum('bqhd,bkhd->bhqk', qi, k, preferred_element_type=jnp.float32) * scale
        if decay is not None:
            s = s + args[2][..., None] - ck[:, :, None, :]
        qpos = i * BLOCK + jnp.arange(BLOCK)
        mask = (kpos[None, :] <= qpos[:, None]) & kvalid[None, :]
        s = jnp.where(mask[None, None], s, NEG)
        p = jax.nn.softmax(s, axis=-1)
        return jnp.einsum('bhqk,bkhd->bqhd', p.astype(v.dtype), v)

    out = lax.map(one_block, xs)
    return out.transpose(1, 0, 2, 3, 4).reshape(B, L, H, v.shape[-1])

def fox_mixer(h, w_in, b_f, w_o):
    B, L, _ = h.shape
    hd = FOX_HEADS * FOX_HEAD_DIM
    proj = h @ w_in
    q, k, v, fg = jnp.split(proj, [hd, 2 * hd, 3 * hd], axis=-1)
    q = q.reshape(B, L, FOX_HEADS, FOX_HEAD_DIM)
    k = k.reshape(B, L, FOX_HEADS, FOX_HEAD_DIM)
    v = v.reshape(B, L, FOX_HEADS, FOX_HEAD_DIM)
    log_f = jax.nn.log_sigmoid((fg + b_f).astype(jnp.float32))
    c = jnp.cumsum(log_f, axis=1)
    o = dense_causal_attention(q, k, v, c)
    return o.reshape(B, L, hd) @ w_o

def swa_mixer(h, w_in, sinks, w_o, cos, sin):
    B, L, _ = h.shape
    G = SWA_Q_HEADS // SWA_KV_HEADS
    d = SWA_HEAD_DIM
    nblk = L // BLOCK
    qd, kd = SWA_Q_HEADS * d, SWA_KV_HEADS * d
    q, k, v = jnp.split(h @ w_in, [qd, qd + kd], axis=-1)
    q = partial_rope(q.reshape(B, L, SWA_Q_HEADS, d), cos, sin)
    k = partial_rope(k.reshape(B, L, SWA_KV_HEADS, d), cos, sin)
    v = v.reshape(B, L, SWA_KV_HEADS, d)

    qb = q.reshape(B, nblk, BLOCK, SWA_KV_HEADS, G, d)
    kb = k.reshape(B, nblk, BLOCK, SWA_KV_HEADS, d)
    vb = v.reshape(B, nblk, BLOCK, SWA_KV_HEADS, d)
    pad_blk = ((0, 0), (1, 0), (0, 0), (0, 0), (0, 0))
    kband = jnp.concatenate([jnp.pad(kb, pad_blk)[:, :-1], kb], axis=2)
    vband = jnp.concatenate([jnp.pad(vb, pad_blk)[:, :-1], vb], axis=2)
    kmeta = k[:, PAD:PAD + N_META]
    vmeta = v[:, PAD:PAD + N_META]

    scale = d ** -0.5
    s_band = jnp.einsum('bnqhgd,bnkhd->bnhgqk', qb, kband, preferred_element_type=jnp.float32) * scale
    s_meta = jnp.einsum('bnqhgd,bmhd->bnhgqm', qb, kmeta, preferred_element_type=jnp.float32) * scale

    qpos = jnp.arange(L).reshape(nblk, BLOCK)
    kpos = (jnp.arange(nblk)[:, None] - 1) * BLOCK + jnp.arange(2 * BLOCK)[None, :]
    diff = qpos[:, :, None] - kpos[:, None, :]
    band_mask = (diff >= 0) & (diff < WINDOW) & (kpos[:, None, :] >= PAD + N_META)
    meta_pos = PAD + jnp.arange(N_META)
    meta_mask = meta_pos[None, None, :] <= qpos[:, :, None]
    s_band = jnp.where(band_mask[None, :, None, None], s_band, NEG)
    s_meta = jnp.where(meta_mask[None, :, None, None], s_meta, NEG)

    sink = sinks.astype(jnp.float32).reshape(SWA_KV_HEADS, G)[None, None, :, :, None, None]
    m = jnp.maximum(jnp.maximum(s_band.max(-1, keepdims=True), s_meta.max(-1, keepdims=True)), sink)
    p_band = jnp.exp(s_band - m)
    p_meta = jnp.exp(s_meta - m)
    denom = p_band.sum(-1, keepdims=True) + p_meta.sum(-1, keepdims=True) + jnp.exp(sink - m)
    p_band = (p_band / denom).astype(v.dtype)
    p_meta = (p_meta / denom).astype(v.dtype)
    o = (jnp.einsum('bnhgqk,bnkhd->bnqhgd', p_band, vband)
         + jnp.einsum('bnhgqm,bmhd->bnqhgd', p_meta, vmeta))
    return o.reshape(B, L, qd) @ w_o

def mla_mixer(h, w_a, g_q, g_kv, w_uq, w_ukv, w_o, cos, sin):
    B, L, _ = h.shape
    cq, ckv, kr = jnp.split(h @ w_a, [MLA_Q_LORA, MLA_Q_LORA + MLA_KV_LORA], axis=-1)
    cq = rms_norm(cq, g_q)
    ckv = rms_norm(ckv, g_kv)
    q = (cq @ w_uq).reshape(B, L, MLA_HEADS, MLA_NOPE + MLA_ROPE)
    q_nope, q_rope = jnp.split(q, [MLA_NOPE], axis=-1)
    q_rope = apply_rope(q_rope, cos, sin)
    k_rope = apply_rope(kr[:, :, None, :], cos, sin)
    kv = (ckv @ w_ukv).reshape(B, L, MLA_HEADS, MLA_NOPE + MLA_V)
    k_nope, v = jnp.split(kv, [MLA_NOPE], axis=-1)
    qf = jnp.concatenate([q_nope, q_rope], axis=-1)
    kf = jnp.concatenate([k_nope, jnp.broadcast_to(k_rope, (B, L, MLA_HEADS, MLA_ROPE))], axis=-1)
    o = dense_causal_attention(qf, kf, v)
    return o.reshape(B, L, MLA_HEADS * MLA_V) @ w_o

def conv_glu_ffn(h, w_in, conv_w, conv_b, w_out, valid):
    L = h.shape[1]
    u = (h @ w_in) * valid.astype(h.dtype)[None, :, None]
    up = jnp.pad(u, ((0, 0), (CONV_W - 1, 0), (0, 0)))
    y = conv_b + up[:, 0:L] * conv_w[0]
    for j in range(1, CONV_W):
        y = y + up[:, j:j + L] * conv_w[j]
    g, val = jnp.split(y, 2, axis=-1)
    return (jax.nn.silu(g) * val) @ w_out

def _dense(key, shape, fan_in, gain=1.0):
    return jax.random.normal(key, shape, jnp.float32) * (gain * fan_in ** -0.5)

def setup_inputs(seed: int = 0) -> dict:
    key = jax.random.key(seed)
    ks = jax.random.split(key, 24)
    D = D_MODEL
    beta = DEEPNORM_BETA
    nrm = lambda k, s: jax.random.normal(k, s, jnp.float32)

    x = nrm(ks[0], (BATCH, SEQ, D))
    meta_tokens = nrm(ks[1], (N_META, D))
    ln1_g = 1.0 + 0.01 * nrm(ks[2], (DEPTH, D))
    ln1_b = 0.01 * nrm(ks[3], (DEPTH, D))
    ln2_g = 1.0 + 0.01 * nrm(ks[4], (DEPTH, D))
    ln2_b = 0.01 * nrm(ks[5], (DEPTH, D))

    fhd = FOX_HEADS * FOX_HEAD_DIM
    fox_cols = jnp.concatenate([jnp.ones((2 * fhd,), jnp.float32), jnp.full((fhd,), beta, jnp.float32),
                                jnp.ones((FOX_HEADS,), jnp.float32)])
    fox_w_in = _dense(ks[6], (N_A, D, 3 * fhd + FOX_HEADS), D) * fox_cols
    fox_b_f = FOX_GATE_BIAS + 0.5 * nrm(ks[7], (N_A, FOX_HEADS))
    fox_w_o = _dense(ks[8], (N_A, fhd, D), fhd, beta)

    sqd, skd = SWA_Q_HEADS * SWA_HEAD_DIM, SWA_KV_HEADS * SWA_HEAD_DIM
    swa_cols = jnp.concatenate([jnp.ones((sqd + skd,), jnp.float32), jnp.full((skd,), beta, jnp.float32)])
    swa_w_in = _dense(ks[9], (N_B, D, sqd + 2 * skd), D) * swa_cols
    swa_sinks = 0.5 * nrm(ks[10], (N_B, SWA_Q_HEADS))
    swa_w_o = _dense(ks[11], (N_B, sqd, D), sqd, beta)

    mla_w_a = _dense(ks[12], (N_C, D, MLA_Q_LORA + MLA_KV_LORA + MLA_ROPE), D)
    mla_g_q = 1.0 + 0.01 * nrm(ks[13], (N_C, MLA_Q_LORA))
    mla_g_kv = 1.0 + 0.01 * nrm(ks[14], (N_C, MLA_KV_LORA))
    mla_w_uq = _dense(ks[15], (N_C, MLA_Q_LORA, MLA_HEADS * (MLA_NOPE + MLA_ROPE)), MLA_Q_LORA)
    ukv_cols = jnp.tile(jnp.concatenate([jnp.ones((MLA_NOPE,), jnp.float32),
                                         jnp.full((MLA_V,), beta, jnp.float32)]), MLA_HEADS)
    mla_w_ukv = _dense(ks[16], (N_C, MLA_KV_LORA, MLA_HEADS * (MLA_NOPE + MLA_V)), MLA_KV_LORA) * ukv_cols
    mla_w_o = _dense(ks[17], (N_C, MLA_HEADS * MLA_V, D), MLA_HEADS * MLA_V, beta)

    ffn_w_in = _dense(ks[18], (DEPTH, D, 2 * D_FF), D, beta)
    ffn_conv_w = _dense(ks[19], (DEPTH, CONV_W, 2 * D_FF), CONV_W)
    ffn_conv_b = 0.01 * nrm(ks[20], (DEPTH, 2 * D_FF))
    ffn_w_out = _dense(ks[21], (DEPTH, D_FF, D), D_FF, beta)

    return {"x": x, "meta_tokens": meta_tokens, "ln1_g": ln1_g, "ln1_b": ln1_b, "ln2_g": ln2_g, "ln2_b": ln2_b,
            "fox_w_in": fox_w_in, "fox_b_f": fox_b_f, "fox_w_o": fox_w_o,
            "swa_w_in": swa_w_in, "swa_sinks": swa_sinks, "swa_w_o": swa_w_o,
            "mla_w_a": mla_w_a, "mla_g_q": mla_g_q, "mla_g_kv": mla_g_kv, "mla_w_uq": mla_w_uq,
            "mla_w_ukv": mla_w_ukv, "mla_w_o": mla_w_o,
            "ffn_w_in": ffn_w_in, "ffn_conv_w": ffn_conv_w, "ffn_conv_b": ffn_conv_b, "ffn_w_out": ffn_w_out}

def reference(x, meta_tokens, ln1_g, ln1_b, ln2_g, ln2_b,
              fox_w_in, fox_b_f, fox_w_o,
              swa_w_in, swa_sinks, swa_w_o,
              mla_w_a, mla_g_q, mla_g_kv, mla_w_uq, mla_w_ukv, mla_w_o,
              ffn_w_in, ffn_conv_w, ffn_conv_b, ffn_w_out):
    B, S, D = x.shape
    h = jnp.concatenate([jnp.zeros((B, PAD, D), x.dtype),
                         jnp.broadcast_to(meta_tokens.astype(x.dtype)[None], (B, N_META, D)), x], axis=1)
    L = h.shape[1]
    idx = jnp.arange(L)
    pos = idx - PAD
    valid = idx >= PAD
    cos_p, sin_p = rope_angles(pos, ROPE_DIM, ROPE_THETA)
    cos_m, sin_m = rope_angles(pos, MLA_ROPE, MLA_ROPE_THETA)

    for i in range(DEPTH):
        kind, j = i % N_MIXERS, i // N_MIXERS
        if kind == 0:
            mix = fox_mixer(h, fox_w_in[j], fox_b_f[j], fox_w_o[j])
        elif kind == 1:
            mix = swa_mixer(h, swa_w_in[j], swa_sinks[j], swa_w_o[j], cos_p, sin_p)
        else:
            mix = mla_mixer(h, mla_w_a[j], mla_g_q[j], mla_g_kv[j], mla_w_uq[j], mla_w_ukv[j], mla_w_o[j],
                            cos_m, sin_m)
        h = layer_norm(DEEPNORM_ALPHA * h + mix, ln1_g[i], ln1_b[i])
        ffn = conv_glu_ffn(h, ffn_w_in[i], ffn_conv_w[i], ffn_conv_b[i], ffn_w_out[i], valid)
        h = layer_norm(DEEPNORM_ALPHA * h + ffn, ln2_g[i], ln2_b[i])
    return h[:, BLOCK:]


_drawn_inputs = setup_inputs


def setup_inputs(seed=0):
    import zlib

    import numpy as np

    out = dict(_drawn_inputs(seed))
    spreads = {}
    factors = {'meta_tokens': 3.125,
     'ln1_g': 2.797,
     'ln1_b': 2.877,
     'ln2_g': 2.867,
     'ln2_b': 2.721,
     'fox_b_f': 53.864,
     'swa_sinks': 8.0,
     'swa_w_o': 3.046,
     'mla_w_a': 3.093,
     'mla_g_q': 8.0,
     'mla_g_kv': 8.0,
     'mla_w_uq': 3.913,
     'mla_w_o': 3.049,
     'ffn_conv_b': 8.0}
    for name, (base, spread) in spreads.items():
        noise = np.random.default_rng([zlib.crc32(name.encode()), seed]).standard_normal(out[name].shape)
        drawn = base * np.exp(spread * noise) if base else spread * noise
        out[name] = __import__('jax').numpy.asarray(drawn.astype(out[name].dtype))
    for name, factor in factors.items():
        out[name] = (out[name] * factor).astype(out[name].dtype)
    return out
```

```python
from contextlib import ExitStack

import numpy as np

import concourse.bass as bass
from concourse import mybir

F32 = mybir.dt.float32
F32R = mybir.dt.float32r
ALU = mybir.AluOpType
ACT = mybir.ActivationFunctionType

P = 128
D = 1024
DC = D // P
SEQ = 256
N_META = 16
T = SEQ + N_META
DEPTH = 4
ALPHA = (2.0 * DEPTH) ** 0.25
LN_EPS = 1e-5
RMS_EPS = 1e-6
NEG = -1e30
HEADS = 16
HD = 64
ROPE_DIM = HD // 4
WINDOW = 128
Q_LORA, KV_LORA, MLA_ROPE = 384, 256, 32
D_FF = 2816
FC = D_FF // P
FA = 14
LAT = 8
UNIT = 8 * P
RING = 4
AHEAD = RING - 1
BANKS = 4

CHUNKS = ((0, 16), (16, 144), (144, 272))
SCOL = (0, 16, 160, 432)
SW = SCOL[3]

KINDS = tuple(("fox", "swa", "mla")[i % 3] for i in range(DEPTH))
K_ROWS = {"fox": HD + 1, "swa": HD, "mla": HD + MLA_ROPE}
SCALE = {"fox": HD ** -0.5, "swa": HD ** -0.5, "mla": (HD + MLA_ROPE) ** -0.5}


class Stage:

    def __init__(self, name, panels, units, body=None):
        self.name, self.panels, self.units = name, panels, units
        self.body = body or len(panels)
        self.turns = len(panels) // self.body
        self.body_units = units // self.turns

    def new_units(self, j):
        before = {u for p in self.panels[:j] for u, _, _ in p}
        return sorted({u for u, _, _ in self.panels[j]} - before)


def whole(name, n, body=None):
    return Stage(name, [[(j, k, k) for k in range(DC)] for j in range(n)], n, body)


def parts(name, n, kt, per_unit):
    return Stage(name, [[(j // per_unit, (j % per_unit) * kt + k, k) for k in range(kt)]
                        for j in range(n)], n // per_unit)


DOWN_TILES = (8, 7, 7)


def down(name):
    one = [(u, t, sum(DOWN_TILES[:u]) + t) for u in range(3) for t in range(DOWN_TILES[u])]
    return Stage(name, [[(3 * j + u, t, k) for u, t, k in one] for j in range(DC)], 3 * DC, 4)


MIXER = {
    "fox": [whole("v", 8, 4), whole("q", 8, 4), whole("k", 8, 4), whole("o", 8, 4)],
    "swa": [whole("v", 1), whole("k", 1), whole("q", 8, 4), whole("o", 8, 4)],
    "mla": [whole("a", 6), parts("v", 8, 2, 4), parts("q", 8, 3, 2), parts("r", 4, 3, 2),
            parts("k", 8, 2, 4), whole("o", 8, 4)],
}
FFN = [whole("up", 2 * FC, 4), down("down")]


def plan():
    u = p = 0
    layers = []
    for kind in KINDS:
        stages = {}
        for s in MIXER[kind] + FFN:
            stages[s.name] = (s, u, p)
            u += s.units
            p += len(s.panels)
        layers.append(stages)
    return layers, u, p


LAYERS, N_UNITS, N_PANELS = plan()
ROPES = [sum({"fox": 0, "swa": 1 + 8, "mla": 1 + 4}[k] for k in KINDS[:a + 1]) for a in range(DEPTH)]


def const_columns():
    at, n = {}, 0
    for name, width in (
        ("ident", P), ("ones", P), ("perm_swa", P), ("perm_mla", P),
        ("mask_causal", SW), ("mask_window", SW),
        ("cos_swa", T), ("sin_swa", T), ("cos_mla", T), ("sin_mla", T),
        ("ln", DEPTH * 2 * 2 * DC), ("conv", DEPTH * 2 * FC * 4), ("sinks", HEADS),
        ("gate_b", 2), ("gate_w", 2 * DC * 16), ("rms_g", 5),
    ):
        at[name] = (n, n + width)
        n += width
    return at, n


CONST, N_CONST = const_columns()


def build_program(nc, x, weights, consts, out):
    with ExitStack() as ctx:
        def sb(name, shape, dt=F32):
            return ctx.enter_context(nc.sbuf_tensor(name, shape, dt))

        def sem(name):
            return ctx.enter_context(nc.semaphore(name))

        h = sb("h", [P, DC, T])
        h_hi = sb("h_hi", [P, DC, T], F32R)
        h_lo = sb("h_lo", [P, DC, T], F32R)
        hid_hi = sb("hid_hi", [P, FA, T], F32R)
        hid_lo = sb("hid_lo", [P, FA, T], F32R)
        with nc.sbuf_tensor("hid2", [P, 2, FC - FA, T], F32R) as hid2:
            pass
        keys = sb("keys", [P, HEADS, T])
        q_all = sb("q_all", [P, DC, T])
        q_rope = sb("q_rope", [P, 4, T])
        v_tok = sb("v_tok", [P, 3, D])
        raw = [sb(f"raw{s}", [P, UNIT]) for s in range(RING)]
        w_hi = [sb(f"w_hi{s}", [P, UNIT], F32R) for s in range(RING)]
        w_lo = [sb(f"w_lo{s}", [P, UNIT], F32R) for s in range(RING)]
        cst = sb("cst", [P, N_CONST])
        scores = sb("scores", [P, 2, SW])
        probs = sb("probs", [P, 2, SW])
        pt0 = sb("pt0", [N_META, 2, T])
        pt12 = sb("pt12", [P, 2, 3 * P])
        q_aug = sb("q_aug", [P, 2, T])
        o_tok = sb("o_tok", [P, 3, P])
        stats = sb("stats", [P, 2, 3, 3])
        sink_exp = sb("sink_exp", [P, 2, 3])
        rinv = sb("rinv", [P, 2, 2, 3])
        y = sb("y", [P, 4, T])
        gated = sb("gated", [P, T])
        squares = sb("squares", [P, 2, T])
        total = sb("total", [P, T])
        rstd = sb("rstd", [P, T])
        eps = sb("eps", [P, 2])
        ps = ctx.enter_context(nc.psum_tensor("ps", [P, 8, 512], F32))

        def c(name, rows=P):
            a, b = CONST[name]
            return cst[0:rows, a:b]

        ident, ones = c("ident"), c("ones")
        ln_par = c("ln").rearrange("p (n two k) -> p n two k", two=2, k=DC)
        conv_par = c("conv").rearrange("p (l j w) -> p l j w", l=DEPTH, w=4)
        gate_w = c("gate_w").rearrange("p (n k m) -> p n k m", n=2, k=DC)
        x_view = x.rearrange("k p t -> p k t")

        raw_landed = [sem(f"raw_landed{s}") for s in range(RING)]
        x_landed, const_landed, out_stored = sem("x_landed"), sem("const_landed"), sem("out_stored")
        hi_ready, lo_ready, w_used = sem("hi_ready"), sem("lo_ready"), sem("w_used")
        panel_done, bank_free = sem("panel_done"), sem("bank_free")
        init_done = sem("init_done")
        resid_added, mu_done, centered = sem("resid_added"), sem("mu_done"), sem("centered")
        squared, square_used, std_done = sem("squared"), sem("square_used"), sem("std_done")
        rescaled, norm_hi, affine_done = sem("rescaled"), sem("norm_hi"), sem("affine_done")
        h_ready = sem("h_ready")
        staged, scored, masked, negated = sem("staged"), sem("scored"), sem("masked"), sem("negated")
        exped, transposed, rinv_done = sem("exped"), sem("transposed"), sem("rinv_done")
        pt0_copied, pt12_copied, pv_done = sem("pt0_copied"), sem("pt12_copied"), sem("pv_done")
        o_normed, o_turned, o_hi, o_split = sem("o_normed"), sem("o_turned"), sem("o_hi"), sem("o_split")
        v_turned, v_copied = sem("v_turned"), sem("v_copied")
        ones_row, decay_moved = sem("ones_row"), sem("decay_moved")
        gate_done, gate_act, decay_done = sem("gate_done"), sem("gate_act"), sem("decay_done")
        swapped, roped = sem("swapped"), sem("roped")
        lat_sq, lat_sum, lat_std, lat_scaled, lat_hi, lat_ready = (
            sem(n) for n in ("lat_sq", "lat_sum", "lat_std", "lat_scaled", "lat_hi", "lat_ready"))
        conv_begun, silu_done, gate_mul, hid_hi_done, hid_ready = (
            sem(n) for n in ("conv_begun", "silu_done", "gate_mul", "hid_hi_done", "hid_ready"))
        dve_own, act_own, pool_own = sem("dve_own"), sem("act_own"), sem("pool_own")

        class Own:

            def __init__(self, eng, s):
                self.eng, self.s, self.base, self.k = eng, s, 0, 0
                self.i, self.per, self.looping = 0, 0, False

            def turn(self, i, per, first=0):
                if not self.looping:
                    self.base += self.k
                self.i, self.per, self.k, self.looping = i, per, 0, True
                self.off = self.base - first * per

            def turned(self, turns):
                assert self.k == self.per, (self.k, self.per)
                self.base += turns * self.per
                self.k, self.looping = 0, False

            def link(self, ins):
                ins.then_inc(self.s, 1)
                self.k += 1
                value = self.i * self.per + (self.off + self.k) if self.looping else self.base + self.k
                self.eng.wait_ge(self.s, value)

        def bank(p):
            return ps[:, p % BANKS, 0:T]

        def at(buf, i):
            return buf[:, i, :] if isinstance(i, int) else \
                buf[:, bass.ds(i, 1), :].rearrange("p o t -> p (o t)")

        def turns(eng, n, emit, first=0):
            if n - first == 1:
                emit(first)
            elif n > first:
                with eng.Fori(first, n) as i:
                    emit(i)

        block = ctx.enter_context(nc.Block())

        @block.sync
        def _(sp):
            sp.dma_start(h[:], x_view).then_inc(x_landed, 16)
            sp.dma_start(raw[0][:], weights[0]).then_inc(raw_landed[0], 16)
            sp.dma_start(cst[:], consts).then_inc(const_landed, 16)
            for u in range(1, RING):
                sp.dma_start(raw[u][:], weights[u]).then_inc(raw_landed[u], 16)

            def unit(u, s):
                sp.wait_ge(lo_ready, u - (RING - 1))
                src = weights[u] if isinstance(u, int) else weights[bass.ds(u, 1)].rearrange("a p n -> p (a n)")
                sp.dma_start(raw[s][:], src).then_inc(raw_landed[s], 16)

            full = N_UNITS // RING
            with sp.Fori(1, full) as i:
                for s in range(RING):
                    unit(i * RING + s, s)
            for u in range(full * RING, N_UNITS):
                unit(u, u % RING)

            for chunk in range(DC):
                sp.wait_ge(affine_done, 8 * (2 * DEPTH - 1) + chunk + 1)
                sp.dma_start(out[chunk], h[:, chunk, N_META:T]).then_inc(out_stored, 16)
            sp.wait_ge(out_stored, 16 * DC)

        @block.tensor
        def _(pe):
            def panel(s, u0, p0, i, j, rhs, ready=None):
                pn = i * s.body + (p0 + j)
                b = bank(p0 + j)
                if not (isinstance(pn, int) and pn < BANKS):
                    pe.wait_ge(bank_free, pn - (BANKS - 1))
                tiles = s.panels[j]
                new = set(s.new_units(j))
                for n, (u, t, k) in enumerate(tiles):
                    un = i * s.body_units + (u0 + u)
                    first = u in new
                    if first:
                        pe.wait_ge(lo_ready, un + 1)
                        new.discard(u)
                    if ready is not None and j == 0:
                        ready(k)
                    slot = (u0 + u) % RING
                    whi, wlo = w_hi[slot][:, t * P:(t + 1) * P], w_lo[slot][:, t * P:(t + 1) * P]
                    xhi, xlo = rhs(k)
                    m = pe.matmul(b, whi, xhi, start=n == 0, stop=False)
                    if first and not (isinstance(un, int) and un == 0):
                        m.then_inc(w_used, 1)
                    pe.matmul(b, whi, xlo, start=False, stop=False)
                    m = pe.matmul(b, wlo, xhi, start=False, stop=n == len(tiles) - 1)
                m.then_inc(panel_done, 1)

            def gemm(layer, name, rhs, ready=None, after=None, straight=False):
                s, u0, p0 = LAYERS[layer][name]

                def turn(i):
                    for j in range(s.body):
                        panel(s, u0, p0, i, j, rhs, ready)
                        if after is not None:
                            after(i, j)

                if straight:
                    for i in range(s.turns):
                        turn(i)
                else:
                    turns(pe, s.turns, turn)

            def from_h(k):
                return h_hi[:, k, :], h_lo[:, k, :]

            def from_first(k):
                return hid_hi[:, k, :], hid_lo[:, k, :]

            def from_latent(first):
                return lambda k: (hid_hi[:, LAT + first + k, :], hid_lo[:, LAT + first + k, :])

            def from_hidden(k):
                if k < FA:
                    return hid_hi[:, k, :], hid_lo[:, k, :]
                return hid2[:, 0, k - FA, :], hid2[:, 1, k - FA, :]

            def norm_ready(n):
                return lambda k: pe.wait_ge(h_ready, 8 * n + k + 1)

            n_v = [0]

            def turn_values(layer, n, stage):
                s, _, p0 = LAYERS[layer][stage]
                pe.wait_ge(bank_free, p0 + len(s.panels))
                for m in range(n):
                    b = ps[:, 4 + m % 2]
                    if m >= 2:
                        pe.wait_ge(v_copied, n_v[0] + m - 1)
                    for ch, (a, e) in enumerate(CHUNKS):
                        t = pe.transpose(b[0:e - a, ch * P:(ch + 1) * P], q_all[:, m, a:e], ident)
                    t.then_inc(v_turned, 1)
                n_v[0] += n

            def attention(a, kind):
                rows = K_ROWS[kind]
                h0, p0 = HEADS * a, HEADS // 2 * a

                def step(i, j, scoring=True, turning=True, mixing=True, outputs=True):
                    hn = i * 4 + j
                    s = j % 2
                    if scoring:
                        key = hn // 8 if kind == "swa" else hn
                        pe.wait_ge(staged, hn + (h0 + 1))
                        if not isinstance(hn, int) or hn >= 2:
                            pe.wait_ge(masked, hn + (h0 - 1))
                        for ch, (lo, hi) in enumerate(CHUNKS):
                            qs, kt = max(hi, P) - P, at(keys, key)[0:rows, 0:hi]
                            m = pe.matmul(ps[:, s, SCOL[ch]:SCOL[ch + 1]],
                                          q_aug[0:rows, s, qs:qs + P], kt, start=True, stop=True)
                        m.then_inc(scored, 1)
                    if turning:
                        pe.wait_ge(exped, hn + (h0 - 1))
                        if not isinstance(hn, int) or hn >= 4:
                            pe.wait_ge(pt0_copied, hn + (h0 - 3))
                            pe.wait_ge(pt12_copied, hn + (h0 - 3))
                        s = j % 2
                        b12, b0 = ps[:, 2 + 2 * s], ps[:, 3 + 2 * s]
                        pr = probs[:, s]
                        pe.transpose(b12[:, 0:128], pr[:, 32:160], ident)
                        pe.transpose(b12[:, 128:256], pr[:, 176:304], ident)
                        pe.transpose(b12[:, 256:384], pr[:, 304:432], ident)
                        pe.transpose(b0[0:16, 0:16], pr[0:16, 0:16], ident[0:16, 0:16])
                        pe.transpose(b0[0:16, 16:144], pr[:, 16:32], ident)
                        pe.transpose(b0[0:16, 144:272], pr[:, 160:176], ident).then_inc(transposed, 1)
                    if mixing:
                        h3 = hn - 3
                        s = (j - 3) % 2
                        col = (h3 // 8 if kind == "swa" else h3) * HD
                        pe.wait_ge(pt0_copied, hn + (h0 - 2))
                        pe.wait_ge(pt12_copied, hn + (h0 - 2))
                        if s == 0 and (not isinstance(hn, int) or hn >= 5):
                            pe.wait_ge(o_normed, i * 2 + ((j - 3) // 2 + p0))

                        def val(ch, rws):
                            if isinstance(col, int):
                                return v_tok[0:rws, ch, col:col + HD]
                            return v_tok[0:rws, ch, bass.ds(col, HD)]

                        o = s * HD
                        ob = ps[:, 6]
                        p0t, p12 = pt0[:, s], pt12[:, s]
                        pe.matmul(ob[:, o:o + HD], p0t[:, 0:P], val(0, 16), start=True, stop=True)
                        pe.matmul(ob[:, P + o:P + o + HD], p0t[:, 16:144], val(0, 16), start=True, stop=False)
                        pe.matmul(ob[:, P + o:P + o + HD], p12[:, 0:128], val(1, P), start=False, stop=True)
                        oc = ob[:, 2 * P + o:2 * P + o + HD]
                        pe.matmul(oc, p0t[:, 144:272], val(0, 16), start=True, stop=False)
                        pe.matmul(oc, p12[:, 128:256], val(1, P), start=False, stop=False)
                        pe.matmul(oc, p12[:, 256:384], val(2, P), start=False, stop=True).then_inc(pv_done, 1)
                    if outputs and j % 2:
                        pe.wait_ge(o_normed, i * 2 + ((j - 5) // 2 + p0 + 1))
                        for ch in (2, 1, 0):
                            lo, hi = CHUNKS[ch]
                            m = pe.transpose(ps[:, 7, lo:hi], o_tok[0:hi - lo, ch, :],
                                             ident[0:hi - lo, 0:hi - lo])
                        m.then_inc(o_turned, 1)

                for j in range(4):
                    step(0, j, turning=j >= 2, mixing=j >= 3, outputs=False)
                with pe.Fori(1, 4) as i:
                    for j in range(4):
                        step(i, j)
                for j in range(4):
                    step(4, j, scoring=False, turning=j < 2, mixing=j < 3)

            def norm(n):
                pe.wait_ge(resid_added, 8 * n + 8)
                pe.matmul(ps[:, 5, 0:T], ones, total[:], start=True, stop=True).then_inc(mu_done, 1)
                for k in range(DC):
                    pe.wait_ge(squared, 8 * n + k + 1)
                    pe.matmul(ps[:, 6, 0:T], ones, squares[:, k % 2, :], start=k == 0,
                              stop=k == DC - 1).then_inc(square_used, 1)

            n_swap = [0]
            n_fox = 0
            pe.wait_ge(const_landed, 16)
            for a, kind in enumerate(KINDS):
                nr = norm_ready(2 * a)
                if kind == "fox":
                    gemm(a, "v", from_h, nr, straight=a == 0)
                    turn_values(a, 8, "v")
                    pe.wait_ge(v_copied, n_v[0])
                    gemm(a, "q", from_h)
                    for k in range(DC):
                        m = pe.matmul(ps[0:16, 6, 0:T], gate_w[:, n_fox, k, :], h[:, k, :],
                                      start=k == 0, stop=k == DC - 1)
                    m.then_inc(gate_done, 1)
                    gemm(a, "k", from_h)
                    pe.wait_ge(decay_moved, 16 * (n_fox + 1))
                    pe.wait_ge(ones_row, n_fox + 1)
                    n_fox += 1
                elif kind == "swa":
                    perm = c("perm_swa")
                    gemm(a, "v", from_h, nr)
                    turn_values(a, 1, "v")

                    def swap(src, done):
                        pe.wait_ge(bank_free, done)
                        pe.wait_ge(roped, n_swap[0])
                        pe.matmul(ps[:, 7, 0:T], perm, src, start=True, stop=True).then_inc(swapped, 1)
                        n_swap[0] += 1

                    gemm(a, "k", from_h)
                    swap(q_rope[:, 0, :], LAYERS[a]["k"][2] + 1)
                    base = n_swap[0]
                    pq = LAYERS[a]["q"][2]

                    def after(i, j):
                        pe.wait_ge(bank_free, i * 4 + (pq + j + 1))
                        pe.wait_ge(roped, i * 4 + (base + j))
                        pe.matmul(ps[:, 7, 0:T], perm, at(q_all, i * 4 + j),
                                  start=True, stop=True).then_inc(swapped, 1)

                    gemm(a, "q", from_h, after=after)
                    n_swap[0] += 8
                else:
                    perm = c("perm_mla")
                    gemm(a, "a", from_h, nr)
                    pe.wait_ge(bank_free, LAYERS[a]["a"][2] + 6)
                    pe.wait_ge(roped, n_swap[0])
                    pe.matmul(ps[:, 7, 0:T], perm, q_all[:, 5, :], start=True, stop=True).then_inc(swapped, 1)
                    n_swap[0] += 1
                    for k in range(5):
                        pe.wait_ge(lat_sq, k + 1)
                        pe.matmul(ps[:, 5 if k < 3 else 6, 0:T], ones, y[:, k % 4, :],
                                  start=k in (0, 3), stop=k in (2, 4)).then_inc(lat_sum, 1)
                    pe.wait_ge(lat_ready, 5)
                    gemm(a, "v", from_latent(3))
                    turn_values(a, 8, "v")
                    pe.wait_ge(v_copied, n_v[0])
                    gemm(a, "q", from_latent(0))
                    pr = LAYERS[a]["r"][2]
                    base = n_swap[0]

                    def after(i, j):
                        pe.wait_ge(bank_free, pr + j + 1)
                        pe.wait_ge(roped, base + j)
                        pe.matmul(ps[:, 7, 0:T], perm, q_rope[:, j, :], start=True, stop=True).then_inc(swapped, 1)

                    gemm(a, "r", from_latent(0), after=after)
                    n_swap[0] += 4
                    gemm(a, "k", from_latent(3))
                pe.wait_ge(v_copied, n_v[0])
                pe.wait_ge(bank_free, LAYERS[a]["o"][2])
                if ROPES[a]:
                    pe.wait_ge(roped, ROPES[a])
                attention(a, kind)
                pe.wait_ge(o_split, 8 * (a + 1))
                gemm(a, "o", from_first)
                norm(2 * a)
                gemm(a, "up", from_h, norm_ready(2 * a + 1))
                gemm(a, "down", from_hidden, ready=lambda k: pe.wait_ge(hid_ready, FC * a + k + 1),
                     straight=a == DEPTH - 1)
                norm(2 * a + 1)

        @block.scalar
        def _(act):
            own = Own(act, act_own)

            def split_hi(u):
                u, slot, rounds = u
                act.wait_ge(raw_landed[slot], rounds * 16)
                if not (isinstance(u, int) and u < RING):
                    act.wait_ge(w_used, u - (RING - 1))
                act.activation(w_hi[slot][:], raw[slot][:], ACT.Copy).then_inc(hi_ready, 1)

            def units_of(layer, name, i, j):
                s, u0, _ = LAYERS[layer][name]
                for u in s.new_units(j):
                    first = u0 + u + AHEAD
                    if isinstance(i, int) and i * s.body_units + first >= N_UNITS:
                        continue
                    yield (i * s.body_units + first, first % RING,
                           i * (s.body_units // RING) + (first // RING + 1)
                           if s.turns > 1 else first // RING + 1)

            def gemm(layer, name, evac=None, links=0, straight=False):
                s, _, p0 = LAYERS[layer][name]

                def turn(i):
                    own.turn(i, links)
                    for j in range(s.body):
                        for u in units_of(layer, name, i, j):
                            split_hi(u)
                        if evac is not None:
                            evac(i, j, i * s.body + (p0 + j))

                if straight:
                    for i in range(s.turns):
                        turn(i)
                else:
                    turns(act, s.turns, turn)
                own.turned(s.turns)

            n_v = [0]

            def copy_values(n):
                for m in range(n):
                    act.wait_ge(v_turned, n_v[0] + m + 1)
                    b = ps[:, 4 + m % 2]
                    act.activation(v_tok[0:16, 0, m * P:(m + 1) * P], b[0:16, 0:P], ACT.Copy)
                    act.activation(v_tok[:, 1:3, m * P:(m + 1) * P],
                                   b[:, P:3 * P].rearrange("p (c n) -> p c n", c=2), ACT.Copy).then_inc(v_copied, 1)
                n_v[0] += n

            def attention(a, kind):
                h0, p0 = HEADS * a, HEADS // 2 * a
                scale = SCALE[kind]

                def step(i, j, staging=True, exping=True, copying=True, outputs=True):
                    hn = i * 4 + j
                    if staging:
                        s = j % 2
                        if not isinstance(hn, int) or hn >= 2:
                            act.wait_ge(scored, hn + (h0 - 1))
                        r = 64 * (j % 2)
                        src = at(q_all, i * 2 + j // 2)[r:r + 64]
                        ins = act.activation(q_aug[0:64, s, :], src, ACT.Copy, scale=scale)
                        if kind == "mla":
                            src = at(q_rope, i)[32 * j:32 * j + 32]
                            ins = act.activation(q_aug[64:96, s, :], src, ACT.Copy, scale=scale)
                        ins.then_inc(staged, 1)
                    if exping:
                        s = (j - 1) % 2
                        act.wait_ge(negated, hn + h0)
                        if not isinstance(hn, int) or hn >= 3:
                            act.wait_ge(transposed, hn + (h0 - 2))
                            act.wait_ge(rinv_done, hn + (h0 - 2))
                        if kind == "swa":
                            h1 = hn - 1
                            a0, _ = CONST["sinks"]
                            sk = cst[:, a0 + h1:a0 + h1 + 1] if isinstance(h1, int) else cst[:, bass.ds(h1 + a0, 1)]
                            act.activation(sink_exp[:, s, :], stats[:, s, 1, :], ACT.Exp, bias=sk)
                        for ch, (lo, hi) in enumerate(CHUNKS):
                            r, cols = hi - lo, slice(SCOL[ch], SCOL[ch + 1])
                            ins = act.activation(probs[0:r, s, cols], scores[0:r, s, cols], ACT.Exp,
                                                 bias=stats[0:r, s, 1, ch:ch + 1],
                                                 accum_out=stats[0:r, s, 2, ch:ch + 1])
                        ins.then_inc(exped, 1)
                    if copying:
                        s = j % 2
                        act.wait_ge(transposed, hn + (h0 - 1))
                        if not isinstance(hn, int) or hn >= 4:
                            act.wait_ge(pv_done, hn + (h0 - 3))
                        act.activation(pt0[:, s, :], ps[0:16, 3 + 2 * s, 0:T], ACT.Copy).then_inc(pt0_copied, 1)
                    if outputs and j % 2 == 1:
                        act.wait_ge(o_turned, i * 2 + (p0 + (j - 5) // 2 + 1))
                        act.activation(at(hid_hi, i * 2 + (j - 5) // 2), ps[:, 7, 0:T],
                                       ACT.Copy).then_inc(o_hi, 1)

                for j in range(4):
                    step(0, j, exping=j >= 1, copying=j >= 2, outputs=False)
                with act.Fori(1, 4) as i:
                    for j in range(4):
                        step(i, j)
                for j in range(4):
                    step(4, j, staging=False, exping=j < 1, copying=j < 2)

            def norm(n):
                for k in range(DC):
                    act.wait_ge(centered, 8 * n + k + 1)
                    if n or k >= 2:
                        act.wait_ge(square_used, 8 * n + k - 1)
                    act.activation(squares[:, k % 2, :], h[:, k, :], ACT.Square).then_inc(squared, 1)
                act.wait_ge(square_used, 8 * n + 8)
                act.activation(rstd[:], ps[:, 6, 0:T], ACT.Sqrt, bias=eps[:, 0:1]).then_inc(std_done, 1)
                last = n == 2 * DEPTH - 1
                for k in range(DC if not last else 0):
                    act.wait_ge(rescaled, 8 * n + k + 1)
                    act.activation(h_hi[:, k, :], h[:, k, :], ACT.Identity, scale=ln_par[:, n, 0, k:k + 1],
                                   bias=ln_par[:, n, 1, k:k + 1]).then_inc(norm_hi, 1)

            act.wait_ge(x_landed, 16)
            for k in range(DC):
                act.activation(h_hi[:, k, :], h[:, k, :], ACT.Copy).then_inc(norm_hi, 1)
            for u in range(AHEAD):
                split_hi((u, u, 1))
            act.wait_ge(const_landed, 16)
            act.wait_ge(init_done, 3)
            n_fox = 0
            for a, kind in enumerate(KINDS):
                if kind == "fox":
                    gemm(a, "v", straight=a == 0)
                    copy_values(8)
                    gemm(a, "q")
                    z, mag, e, u1, lnu = (y[0:16, 0, :], y[0:16, 1, :], y[0:16, 2, :], y[0:16, 3, :], gated[0:16, :])
                    act.wait_ge(gate_done, n_fox + 1)
                    gb = CONST["gate_b"][0] + n_fox
                    bias = cst[0:16, gb:gb + 1]
                    act.activation(z, ps[0:16, 6, 0:T], ACT.Identity, bias=bias)
                    own.link(act.activation(mag, ps[0:16, 6, 0:T], ACT.Abs, bias=bias))
                    own.link(act.activation(e, mag, ACT.Exp, scale=-1.0))
                    own.link(act.activation(u1, e, ACT.Identity, bias=1.0))
                    act.activation(lnu, u1, ACT.Ln).then_inc(gate_act, 1)
                    gemm(a, "k")
                    n_fox += 1
                elif kind == "swa":
                    gemm(a, "v")
                    copy_values(1)
                    gemm(a, "k")
                    gemm(a, "q")
                else:
                    gemm(a, "a")
                    pa = LAYERS[a]["a"][2]
                    act.wait_ge(bank_free, pa + 5)
                    for k in range(5):
                        if k >= 4:
                            act.wait_ge(lat_sum, k - 3)
                        act.activation(y[:, k % 4, :], q_all[:, k, :], ACT.Square).then_inc(lat_sq, 1)
                    for k, (width, at_sum) in enumerate(((Q_LORA, 3), (KV_LORA, 5))):
                        act.wait_ge(lat_sum, at_sum)
                        act.activation(squares[:, k, :], ps[:, 5 + k, 0:T], ACT.Sqrt, scale=float(D) / width,
                                       bias=eps[:, 1:2]).then_inc(lat_std, 1)
                    g0 = CONST["rms_g"][0]
                    for k in range(5):
                        act.wait_ge(lat_scaled, k + 1)
                        act.activation(hid_hi[:, LAT + k, :], q_all[:, k, :], ACT.Identity,
                                       scale=cst[:, g0 + k:g0 + k + 1]).then_inc(lat_hi, 1)
                    gemm(a, "v")
                    copy_values(8)
                    gemm(a, "q")
                    gemm(a, "r")
                    gemm(a, "k")
                act.wait_ge(bank_free, LAYERS[a]["o"][2])
                if ROPES[a]:
                    act.wait_ge(roped, ROPES[a])
                attention(a, kind)
                gemm(a, "o")
                norm(2 * a)

                def up(i, j, pn):
                    pr, which = j // 2, j % 2
                    s = 2 * pr + which
                    idx = i * 4 + j
                    par = conv_par[:, a]
                    col = (lambda w: par[:, idx, w:w + 1]) if isinstance(idx, int) else \
                        (lambda w: par[:, bass.ds(idx, 1), w])
                    act.wait_ge(panel_done, pn + 1)
                    act.activation(y[:, s, :], bank(LAYERS[a]["up"][2] + j), ACT.Identity,
                                   scale=col(2), bias=col(3)).then_inc(conv_begun, 1)
                    if which:
                        cn = i * 2 + (FC * a + pr)
                        act.wait_ge(bank_free, pn)
                        act.activation(y[:, s - 1, :], y[:, s - 1, :], ACT.Silu).then_inc(silu_done, 1)
                        act.wait_ge(gate_mul, cn + 1)
                        dst = up_dst[0](i, pr)
                        act.activation(dst, gated[:], ACT.Copy).then_inc(hid_hi_done, 1)

                up_dst = [None]
                s, _, p0 = LAYERS[a]["up"]

                def up_turn(i):
                    for j in range(4):
                        for u in units_of(a, "up", i, j):
                            split_hi(u)
                        up(i, j, i * 4 + (p0 + j))

                up_dst[0] = lambda i, pr: at(hid_hi, i * 2 + pr)
                turns(act, FA // 2, up_turn)
                up_dst[0] = lambda i, pr: at(hid2[:, 0], i * 2 + (pr - FA))
                turns(act, FC // 2, up_turn, first=FA // 2)
                gemm(a, "down", straight=a == DEPTH - 1)
                norm(2 * a + 1)

        @block.gpsimd
        def _(pool):
            own = Own(pool, pool_own)
            pool.memset(eps[:, 0:1], LN_EPS).then_inc(init_done, 1)
            pool.memset(eps[:, 1:2], RMS_EPS).then_inc(init_done, 1)
            pool.memset(stats[:], 1.0).then_inc(init_done, 1)

            def norm(n, stage):
                _, _, p0 = LAYERS[n // 2][stage]
                if n:
                    pool.wait_ge(mu_done, n)
                own.link(pool.memset(total[:], 0.0))
                for k in range(DC):
                    pool.wait_ge(bank_free, p0 + k + 1)
                    pool.tensor_tensor(total[:], total[:], h[:, k, :], ALU.add).then_inc(resid_added, 1)
                    pool.wait_ge(resid_added, 8 * n + k + 1)
                last = n == 2 * DEPTH - 1
                for k in range(DC):
                    if last:
                        pool.wait_ge(rescaled, 8 * n + k + 1)
                    else:
                        pool.wait_ge(norm_hi, 8 * (n + 1) + k + 1)
                    pool.tensor_scalar(h[:, k, :], h[:, k, :], ln_par[:, n, 0, k:k + 1],
                                       ln_par[:, n, 1, k:k + 1], ALU.mult, ALU.add).then_inc(affine_done, 1)

            n_fox = 0
            pool.wait_ge(init_done, 3)
            pool.wait_ge(const_landed, 16)
            for a, kind in enumerate(KINDS):
                if kind == "fox":
                    pool.wait_ge(decay_done, n_fox + 1)
                    pool.dma_start(keys[64:65, :, :], y[0:16, 1, :]).then_inc(decay_moved, 16)
                    pool.wait_ge(decay_moved, 16 * (n_fox + 1))
                    n_fox += 1
                norm(2 * a, "o")
                norm(2 * a + 1, "down")

        @block.vector
        def _(dve):
            own = Own(dve, dve_own)
            copy = dve.tensor_copy

            def tt(out_, a_, b_, op):
                return dve.tensor_tensor(out_, a_, b_, op)

            def split_lo(u, slot):
                dve.wait_ge(hi_ready, u + 1)
                tt(w_lo[slot][:], raw[slot][:], w_hi[slot][:].bitcast(F32), ALU.subtract).then_inc(lo_ready, 1)

            def split_units(layer, name, i, j):
                s, u0, _ = LAYERS[layer][name]
                for u in s.new_units(j):
                    first = u0 + u + AHEAD
                    if isinstance(i, int) and i * s.body_units + first >= N_UNITS:
                        continue
                    split_lo(i * s.body_units + first, first % RING)

            def gemm(layer, name, evac, links=0, straight=False):
                s, _, p0 = LAYERS[layer][name]

                def turn(i):
                    own.turn(i, links)
                    for j in range(s.body):
                        split_units(layer, name, i, j)
                        dve.wait_ge(panel_done, i * s.body + (p0 + j + 1))
                        evac(i, j, bank(p0 + j), i * s.body + (p0 + j))

                if straight:
                    for i in range(s.turns):
                        turn(i)
                else:
                    turns(dve, s.turns, turn)
                own.turned(s.turns)

            def to_q(body):
                def evac(i, j, b, pn):
                    copy(at(q_all, i * body + j), b).then_inc(bank_free, 1)
                return evac

            def to_keys(body):
                def evac(i, j, b, pn):
                    m2 = i * (2 * body) + 2 * j
                    copy(keys_at(m2), b[0:64])
                    copy(keys_at(m2 + 1), b[64:128]).then_inc(bank_free, 1)
                return evac

            def keys_at(n):
                return at(keys, n)[0:64]

            def rope(qn, swap_no, cos, sin, dst, rows=P):
                tt(y[0:rows, 0, :], qn[0:rows], cos[0:rows], ALU.mult)
                dve.wait_ge(swapped, swap_no)
                own.link(tt(y[0:rows, 1, :], ps[0:rows, 7, 0:T], sin[0:rows], ALU.mult))
                return tt(dst, y[0:rows, 0, :], y[0:rows, 1, :], ALU.add)

            def attention(a, kind):
                h0, p0 = HEADS * a, HEADS // 2 * a
                mask = c("mask_window" if kind == "swa" else "mask_causal")

                def step(i, j, masking=True, copying=True, summing=True, norming=True, splitting=True):
                    hn = i * 4 + j
                    if copying:
                        s = j % 2
                        dve.wait_ge(transposed, hn + (h0 - 1))
                        if not isinstance(hn, int) or hn >= 4:
                            dve.wait_ge(pv_done, hn + (h0 - 3))
                        copy(pt12[:, s, :], ps[:, 2 + 2 * s, 0:3 * P]).then_inc(pt12_copied, 1)
                    if masking:
                        s = j % 2
                        if not copying:
                            dve.wait_ge(scored, hn + (h0 + 1))
                        for ch, (lo, hi) in enumerate(CHUNKS):
                            r, cols = hi - lo, slice(SCOL[ch], SCOL[ch + 1])
                            ins = dve.tensor_tensor_reduce(
                                out=scores[0:r, s, cols], in0=ps[0:r, s, cols], in1=mask[0:r, cols],
                                scale=1.0, scalar=-3.0e38, op0=ALU.add, op1=ALU.max,
                                accum_out=stats[0:r, s, 0, ch:ch + 1])
                        ins.then_inc(masked, 1)
                        dve.wait_ge(masked, hn + (h0 + 1))
                        if kind == "swa":
                            a0, _ = CONST["sinks"]
                            sk = cst[:, a0 + hn:a0 + hn + 1] if isinstance(hn, int) else cst[:, bass.ds(hn + a0, 1)]
                            dve.tensor_scalar(stats[:, s, 1, :], stats[:, s, 0, :], sk, -1.0,
                                              ALU.max, ALU.mult).then_inc(negated, 1)
                        else:
                            dve.tensor_scalar(stats[:, s, 1, :], stats[:, s, 0, :], -1.0, None,
                                              ALU.mult).then_inc(negated, 1)
                    if summing:
                        s = j % 2
                        pp = ((j - 2) // 2) % 2
                        dve.wait_ge(exped, hn + (h0 - 1))
                        if kind == "swa":
                            own.link(tt(stats[:, s, 2, :], stats[:, s, 2, :], sink_exp[:, s, :], ALU.add))
                        dve.reciprocal(rinv[:, pp, j % 2, :], stats[:, s, 2, :]).then_inc(rinv_done, 1)
                    if norming and j % 2 == 0:
                        pair = i * 2 + (j - 4) // 2
                        pp = ((j - 4) // 2) % 2
                        dve.wait_ge(rinv_done, hn + (h0 - 2))
                        dve.wait_ge(pv_done, hn + (h0 - 2))
                        for ch, (lo, hi) in enumerate(CHUNKS):
                            r = hi - lo
                            ri = rinv[0:r, pp, :, ch:ch + 1].broadcast_to([r, 2, HD])
                            ins = tt(o_tok[0:r, ch, :].rearrange("p (n d) -> p n d", n=2),
                                     ps[0:r, 6, ch * P:(ch + 1) * P].rearrange("p (n d) -> p n d", n=2),
                                     ri, ALU.mult)
                        ins.then_inc(o_normed, 1)
                    if splitting and j % 2 == 1:
                        pair = i * 2 + (j - 5) // 2
                        dve.wait_ge(o_hi, pair + (p0 + 1))
                        tt(at(hid_lo, pair), ps[:, 7, 0:T], at(hid_hi, pair).bitcast(F32),
                           ALU.subtract).then_inc(o_split, 1)

                links = 4 if kind == "swa" else 0
                for j in range(4):
                    step(0, j, copying=j >= 2, summing=j >= 2, norming=False, splitting=False)
                with dve.Fori(1, 4) as i:
                    own.turn(i, links, first=1)
                    for j in range(4):
                        step(i, j)
                own.turned(3)
                for j in range(4):
                    step(4, j, masking=False, copying=j < 2, summing=j < 2, norming=j < 3)

            def residual(i, j, b, pn, body=4):
                hk = at(h, i * body + j)
                dve.scalar_tensor_tensor(hk, hk, ALPHA, b, ALU.mult, ALU.add).then_inc(bank_free, 1)

            def norm(n):
                last = n == 2 * DEPTH - 1
                dve.wait_ge(mu_done, n + 1)
                for k in range(DC):
                    tt(h[:, k, :], h[:, k, :], ps[:, 5, 0:T], ALU.subtract).then_inc(centered, 1)
                dve.wait_ge(std_done, n + 1)
                own.link(dve.reciprocal(rstd[:], rstd[:]))

                def lo_part(k):
                    dve.wait_ge(affine_done, 8 * n + k + 1)
                    tt(h_lo[:, k, :], h[:, k, :], h_hi[:, k, :].bitcast(F32), ALU.subtract).then_inc(h_ready, 1)

                for k in range(DC):
                    dve.wait_ge(squared, 8 * n + k + 1)
                    tt(h[:, k, :], h[:, k, :], rstd[:], ALU.mult).then_inc(rescaled, 1)
                    if k >= 3 and not last:
                        lo_part(k - 3)
                if not last:
                    for k in range(DC - 3, DC):
                        lo_part(k)

            for k in range(DC):
                dve.wait_ge(norm_hi, k + 1)
                tt(h_lo[:, k, :], h[:, k, :], h_hi[:, k, :].bitcast(F32), ALU.subtract).then_inc(h_ready, 1)
            for u in range(AHEAD):
                split_lo(u, u)
            dve.wait_ge(const_landed, 16)
            dve.wait_ge(init_done, 3)
            n_fox, n_swap, n_v = 0, 0, 0
            for a, kind in enumerate(KINDS):
                if kind == "fox":
                    if a:
                        dve.wait_ge(scored, HEADS * a)
                    dve.memset(q_aug[64:65, :, :], 1.0).then_inc(ones_row, 1)
                    gemm(a, "v", to_q(4))
                    n_v += 8
                    dve.wait_ge(v_turned, n_v)
                    gemm(a, "q", to_q(4))
                    z, mag, e, u1, lnu = (y[0:16, 0, :], y[0:16, 1, :], y[0:16, 2, :], y[0:16, 3, :], gated[0:16, :])
                    zero = squares[0:16, 0, :]
                    dve.wait_ge(gate_act, n_fox + 1)
                    own.link(dve.tensor_scalar(u1, u1, -1.0, None, ALU.add))
                    own.link(dve.tensor_scalar(zero, u1, 0.0, None, ALU.is_equal))
                    tt(lnu, lnu, zero, ALU.add)
                    own.link(tt(u1, u1, zero, ALU.add))
                    own.link(dve.reciprocal(u1, u1))
                    own.link(tt(lnu, lnu, u1, ALU.mult))
                    own.link(tt(lnu, lnu, e, ALU.mult))
                    own.link(dve.tensor_scalar(z, z, -1.0, 0.0, ALU.mult, ALU.max))
                    own.link(tt(lnu, lnu, z, ALU.add))
                    own.link(dve.tensor_scalar(zero, zero, 0.0, 1.0, ALU.mult, ALU.add))
                    dve.tensor_tensor_scan(mag, zero, lnu, 0.0, ALU.mult, ALU.add).then_inc(decay_done, 1)
                    gemm(a, "k", to_keys(4))
                    n_fox += 1
                elif kind == "swa":
                    cos, sin = c("cos_swa"), c("sin_swa")
                    gemm(a, "v", to_q(1))
                    n_v += 1

                    def k_evac(i, j, b, pn):
                        copy(q_rope[:, 0, :], b).then_inc(bank_free, 1)
                        dve.wait_ge(bank_free, pn + 1)

                    gemm(a, "k", k_evac)
                    n_swap += 1
                    own.link(rope(q_rope[:, 0, :], n_swap, cos, sin, q_rope[:, 0, :]))
                    copy(keys[0:64, 0, :], q_rope[0:64, 0, :])
                    copy(keys[0:64, 1, :], q_rope[64:128, 0, :]).then_inc(roped, 1)
                    dve.wait_ge(v_turned, n_v)
                    base = n_swap

                    def q_evac(i, j, b, pn):
                        qn = at(q_all, i * 4 + j)
                        copy(qn, b).then_inc(bank_free, 1)
                        dve.wait_ge(bank_free, pn + 1)
                        if isinstance(i, int):
                            dve.wait_ge(roped, base + i * 4 + j)
                        else:
                            dve.wait_ge(roped, i * 4 + (base + j))
                        rope(qn, i * 4 + (base + j + 1), cos, sin, qn).then_inc(roped, 1)

                    gemm(a, "q", q_evac, links=4)
                    n_swap += 8
                else:
                    cos, sin = c("cos_mla"), c("sin_mla")
                    gemm(a, "a", to_q(6))
                    n_swap += 1
                    pa = LAYERS[a]["a"][2]
                    dve.wait_ge(bank_free, pa + 6)
                    own.link(tt(scores[0:32, 0, 0:T], q_all[0:32, 5, :], cos[0:32], ALU.mult))
                    dve.wait_ge(swapped, n_swap)
                    own.link(tt(scores[0:32, 1, 0:T], ps[0:32, 7, 0:T], sin[0:32], ALU.mult))
                    own.link(tt(scores[0:32, 0, 0:T], scores[0:32, 0, 0:T], scores[0:32, 1, 0:T], ALU.add))
                    copy(keys[64:96, :, :], scores[0:32, 0, 0:T].unsqueeze(1).broadcast_to([32, HEADS, T])).then_inc(roped, 1)
                    g0 = CONST["rms_g"][0]
                    for k in range(5):
                        buf = squares[:, k // 3, :]
                        if k in (0, 3):
                            dve.wait_ge(lat_std, 1 + k // 3)
                            own.link(dve.reciprocal(buf, buf))
                        dve.wait_ge(lat_sq, k + 1)
                        tt(q_all[:, k, :], q_all[:, k, :], buf, ALU.mult).then_inc(lat_scaled, 1)
                        dve.wait_ge(lat_hi, k + 1)
                        dve.scalar_tensor_tensor(hid_lo[:, LAT + k, :], q_all[:, k, :], cst[:, g0 + k:g0 + k + 1],
                                                 hid_hi[:, LAT + k, :].bitcast(F32), ALU.mult,
                                                 ALU.subtract).then_inc(lat_ready, 1)
                    gemm(a, "v", to_q(8))
                    n_v += 8
                    dve.wait_ge(v_turned, n_v)
                    gemm(a, "q", to_q(8))
                    base = n_swap

                    def r_evac(i, j, b, pn):
                        qn = q_rope[:, j, :]
                        copy(qn, b).then_inc(bank_free, 1)
                        dve.wait_ge(bank_free, pn + 1)
                        dve.wait_ge(roped, base + j)
                        rope(qn, base + j + 1, cos, sin, qn).then_inc(roped, 1)

                    gemm(a, "r", r_evac, links=4)
                    n_swap += 4
                    gemm(a, "k", to_keys(8))
                attention(a, kind)
                gemm(a, "o", residual)
                norm(2 * a)

                def up_turn_of(dst_lo, dst_hi):
                    def turn(i):
                        own.turn(i, 4)
                        p0 = LAYERS[a]["up"][2]
                        for j in range(4):
                            split_units(a, "up", i, j)
                            b = bank(p0 + j)
                            idx = i * 4 + j
                            par = conv_par[:, a]
                            col = (lambda w: par[:, idx, w:w + 1]) if isinstance(idx, int) else \
                                (lambda w: par[:, bass.ds(idx, 1), w])
                            yj = y[:, j, :]
                            dve.wait_ge(conv_begun, i * 4 + (2 * FC * a + j + 1))
                            own.link(dve.scalar_tensor_tensor(yj[:, 1:T], b[:, 0:T - 1], col(1), yj[:, 1:T],
                                                              ALU.mult, ALU.add))
                            dve.scalar_tensor_tensor(yj[:, 2:T], b[:, 0:T - 2], col(0), yj[:, 2:T],
                                                     ALU.mult, ALU.add).then_inc(bank_free, 1)
                            if j % 2:
                                pr = j // 2
                                cn = i * 2 + (FC * a + pr)
                                dve.wait_ge(bank_free, i * 4 + (p0 + j + 1))
                                dve.wait_ge(silu_done, cn + 1)
                                tt(gated[:], y[:, j - 1, :], yj, ALU.mult).then_inc(gate_mul, 1)
                                dve.wait_ge(hid_hi_done, cn + 1)
                                tt(dst_lo(i, pr), gated[:], dst_hi(i, pr).bitcast(F32),
                                   ALU.subtract).then_inc(hid_ready, 1)
                    return turn

                turns(dve, FA // 2, up_turn_of(lambda i, pr: at(hid_lo, i * 2 + pr),
                                               lambda i, pr: at(hid_hi, i * 2 + pr)))
                turns(dve, FC // 2, up_turn_of(lambda i, pr: at(hid2[:, 1], i * 2 + (pr - FA)),
                                               lambda i, pr: at(hid2[:, 0], i * 2 + (pr - FA))),
                      first=FA // 2)
                own.turned(FC // 2)
                gemm(a, "down", residual, straight=a == DEPTH - 1)
                norm(2 * a + 1)



def panels(w):
    k, n = w.shape
    return w.reshape(k // P, P, n // P, P).transpose(2, 1, 0, 3)


def units(w, per_unit=1):
    a = panels(w)
    n, _, kt, _ = a.shape
    a = a.reshape(n // per_unit, per_unit, P, kt, P).transpose(0, 2, 1, 3, 4).reshape(n // per_unit, P, -1)
    full = np.zeros((a.shape[0], P, UNIT), a.dtype)
    full[:, :, :a.shape[2]] = a
    return full


def down_units(w):
    a = panels(w)
    full = np.zeros((DC, 3, P, UNIT), w.dtype)
    k = 0
    for u, n in enumerate(DOWN_TILES):
        full[:, u, :, :n * P] = a[:, :, k:k + n].reshape(DC, P, n * P)
        k += n
    return full.reshape(3 * DC, P, UNIT)


def layer_units(a, kind, inp):
    j = a // 3
    if kind == "fox":
        w = inp["fox_w_in"][j]
        mixer = [w[:, 2 * D:3 * D], w[:, :D], w[:, D:2 * D], inp["fox_w_o"][j]]
        mixer = [units(m) for m in mixer]
    elif kind == "swa":
        w = inp["swa_w_in"][j]
        kd = 2 * HD
        mixer = [units(m) for m in (w[:, D + kd:], w[:, D:D + kd], w[:, :D], inp["swa_w_o"][j])]
    else:
        wa = inp["mla_w_a"][j]
        wide = np.zeros((D, 6 * P), wa.dtype)
        wide[:, :wa.shape[1]] = wa
        uq = inp["mla_w_uq"][j].reshape(Q_LORA, HEADS, HD + MLA_ROPE)
        ukv = inp["mla_w_ukv"][j].reshape(KV_LORA, HEADS, 2 * HD)
        mixer = [units(wide), units(ukv[:, :, HD:].reshape(KV_LORA, D), 4),
                 units(uq[:, :, :HD].reshape(Q_LORA, D), 2),
                 units(uq[:, :, HD:].reshape(Q_LORA, HEADS * MLA_ROPE), 2),
                 units(ukv[:, :, :HD].reshape(KV_LORA, D), 4), units(inp["mla_w_o"][j])]
    up = units(inp["ffn_w_in"][a])
    up = np.stack([up[:FC], up[FC:]], 1).reshape(2 * FC, P, UNIT)
    return mixer + [up, down_units(inp["ffn_w_out"][a])]


def rope_tables(dim, theta, period):
    inv = (np.float32(theta) ** (-np.arange(0, dim, 2, dtype=np.float32) / np.float32(dim))).astype(np.float32)
    ang = np.arange(T, dtype=np.float32)[:, None] * inv[None, :]
    cos, sin = np.ones((P, T), np.float32), np.zeros((P, T), np.float32)
    perm = np.zeros((P, P), np.float32)
    half = dim // 2
    for p in range(P):
        d = p % period
        if d < dim:
            cos[p] = np.cos(ang[:, d % half])
            sin[p] = np.sin(ang[:, d % half]) * (-1 if d < half else 1)
            perm[p + half if d < half else p - half, p] = 1.0
    return cos, sin, perm


def masks():
    both = []
    for window in (T, WINDOW):
        m = np.full((P, SW), NEG, np.float32)
        for ch, (lo, hi) in enumerate(CHUNKS):
            q, k = np.arange(lo, hi)[:, None], np.arange(hi)[None, :]
            seen = (k <= q) & ((q - k < window) | (k < N_META))
            m[:hi - lo, SCOL[ch]:SCOL[ch + 1]] = np.where(seen, 0.0, NEG)
        both.append(m)
    return both


def const_block(inp):
    block = np.zeros((P, N_CONST), np.float32)

    def put(name, a, rows=P):
        lo, hi = CONST[name]
        block[:rows, lo:hi] = a.reshape(rows, hi - lo)

    put("ident", np.eye(P, dtype=np.float32))
    put("ones", np.full((P, P), 1.0 / D, np.float32))
    for name, args in (("swa", (ROPE_DIM, 500000.0, HD)), ("mla", (MLA_ROPE, 10000.0, MLA_ROPE))):
        cos, sin, perm = rope_tables(*args)
        put("cos_" + name, cos)
        put("sin_" + name, sin)
        put("perm_" + name, perm)
    causal, window = masks()
    put("mask_causal", causal)
    put("mask_window", window)
    ln = np.stack([np.stack([inp["ln1_g"], inp["ln1_b"]], 1), np.stack([inp["ln2_g"], inp["ln2_b"]], 1)], 1)
    put("ln", ln.reshape(DEPTH * 4, DC, P).transpose(2, 0, 1))
    cv = np.concatenate([inp["ffn_conv_w"], inp["ffn_conv_b"][:, None]], 1)
    put("conv", cv.reshape(DEPTH, 4, 2, FC, P).transpose(4, 0, 3, 2, 1))
    put("sinks", np.broadcast_to(inp["swa_sinks"][0], (P, HEADS)))
    put("gate_b", inp["fox_b_f"].T, HEADS)
    put("gate_w", inp["fox_w_in"][:, :, 3 * D:].reshape(2, DC, P, HEADS).transpose(2, 0, 1, 3))
    g = np.concatenate([inp["mla_g_q"][0], inp["mla_g_kv"][0]])
    put("rms_g", g.reshape(5, P).T)
    return block


def kernel(**inputs):
    import concourse.bacc as bacc
    from concourse.bass_utils import run_bass_kernel_spmd

    inp = {k: np.asarray(v) for k, v in inputs.items()}
    tokens = np.concatenate([inp["meta_tokens"], inp["x"][0]], 0)
    arrays = {
        "in_x": np.ascontiguousarray(tokens.T.reshape(DC, P, T)),
        "in_weights": np.concatenate([u for a, kind in enumerate(KINDS) for u in layer_units(a, kind, inp)], 0),
        "in_consts": const_block(inp),
    }
    assert arrays["in_weights"].shape[0] == N_UNITS
    nc = bacc.Bacc("TRN2", target_bir_lowering=False, num_devices=1)
    args = [nc.dram_tensor(n, a.shape, mybir.dt.from_np(a.dtype), kind="ExternalInput").ap()
            for n, a in arrays.items()]
    out = nc.dram_tensor("out_0", (DC, P, SEQ), F32, kind="ExternalOutput").ap()
    build_program(nc, *args, out)
    got = run_bass_kernel_spmd(nc, [arrays], core_ids=[0]).results[0]["out_0"]
    return np.ascontiguousarray(got.reshape(D, SEQ).T)[None]
```

```python
from contextlib import ExitStack

import numpy as np

import concourse.bass as bass
from concourse import mybir

F32 = mybir.dt.float32
F32R = mybir.dt.float32r
ALU = mybir.AluOpType
ACT = mybir.ActivationFunctionType

P = 128
D = 1024
DC = D // P
SEQ = 256
N_META = 16
T = SEQ + N_META
DEPTH = 4
ALPHA = (2.0 * DEPTH) ** 0.25
LN_EPS = 1e-5
RMS_EPS = 1e-6
NEG = -1e30
HEADS = 16
HD = 64
ROPE_DIM = HD // 4
WINDOW = 128
Q_LORA, KV_LORA, MLA_ROPE = 384, 256, 32
D_FF = 2816
FC = D_FF // P
FA = 13
SPLIT = (FA + 1) // 2
LAT = 8
UNIT = 8 * P
RING = 4
AHEAD = RING - 1
BANKS = 4

CHUNKS = ((0, N_META), (N_META, N_META + P), (N_META + P, T))
SCOL = (0, 16, 160, 432)
SW = SCOL[3]
PCOL = (0, P, 3 * P)
PW = PCOL[2] + T
TAIL = T - 2 * P
PT1, PT2, PTW = T, T + P + TAIL, T + P + 2 * TAIL

KINDS = tuple(("fox", "swa", "mla")[i % 3] for i in range(DEPTH))
K_ROWS = {"fox": HD + 1, "swa": HD, "mla": HD + MLA_ROPE}
SCALE = {"fox": HD ** -0.5, "swa": HD ** -0.5, "mla": (HD + MLA_ROPE) ** -0.5}


class Stage:

    def __init__(self, name, panels, units, body=None):
        self.name, self.panels, self.units = name, panels, units
        self.body = body or len(panels)
        self.turns = len(panels) // self.body
        self.body_units = units // self.turns

    def new_units(self, j):
        before = {u for p in self.panels[:j] for u, _, _ in p}
        return sorted({u for u, _, _ in self.panels[j]} - before)


def whole(name, n, body=None):
    return Stage(name, [[(j, k, k) for k in range(DC)] for j in range(n)], n, body)


def parts(name, n, kt, per_unit):
    return Stage(name, [[(j // per_unit, (j % per_unit) * kt + k, k) for k in range(kt)]
                        for j in range(n)], n // per_unit)


DOWN_TILES = (8, 7, 7)


def down(name):
    one = [(u, t, sum(DOWN_TILES[:u]) + t) for u in range(3) for t in range(DOWN_TILES[u])]
    return Stage(name, [[(3 * j + u, t, k) for u, t, k in one] for j in range(DC)], 3 * DC, 4)


MIXER = {
    "fox": [whole("v", 8, 4), whole("q", 8, 4), whole("k", 8, 4), whole("o", 8, 4)],
    "swa": [whole("v", 1), whole("k", 1), whole("q", 8, 4), whole("o", 8, 4)],
    "mla": [whole("a", 6), parts("v", 8, 2, 4), parts("q", 8, 3, 2), parts("r", 4, 3, 2),
            parts("k", 8, 2, 4), whole("o", 8, 4)],
}
FFN = [whole("up", 2 * FC, 4), down("down")]


def plan():
    u = p = 0
    layers = []
    for kind in KINDS:
        stages = {}
        for s in MIXER[kind] + FFN:
            stages[s.name] = (s, u, p)
            u += s.units
            p += len(s.panels)
        layers.append(stages)
    return layers, u, p


LAYERS, N_UNITS, N_PANELS = plan()
ROPES = [sum({"fox": 0, "swa": 1 + 8, "mla": 1 + 4}[k] for k in KINDS[:a + 1]) for a in range(DEPTH)]


def const_columns():
    at, n = {}, 0
    for name, width in (
        ("ident", P), ("ones", P), ("perm_swa", P), ("perm_mla", P),
        ("mask_causal", SW), ("mask_window", SW),
        ("cos_swa", T), ("sin_swa", T), ("cos_mla", T), ("sin_mla", T),
        ("ln", DEPTH * 2 * 2 * DC), ("conv", DEPTH * 2 * FC * 4), ("sinks", HEADS),
        ("gate_b", 2), ("gate_w", 2 * DC * 16), ("rms_g", 5),
    ):
        at[name] = (n, n + width)
        n += width
    return at, n


CONST, N_CONST = const_columns()


def build_program(nc, x, weights, consts, out):
    with ExitStack() as ctx:
        def sb(name, shape, dt=F32):
            return ctx.enter_context(nc.sbuf_tensor(name, shape, dt))

        def sem(name):
            return ctx.enter_context(nc.semaphore(name))

        h = sb("h", [P, DC, T])
        h_hi = sb("h_hi", [P, DC, T], F32R)
        h_lo = sb("h_lo", [P, DC, T], F32R)
        hid_hi = sb("hid_hi", [P, FA, T], F32R)
        hid_lo = sb("hid_lo", [P, FA, T], F32R)
        with nc.sbuf_tensor("keys", [P, HEADS, T], F32) as keys:
            pass
        hid2 = sb("hid2", [P, 2, FC - FA, T], F32R)
        q_all = sb("q_all", [P, DC, T])
        q_rope = sb("q_rope", [P, 4, T])
        v_tok = sb("v_tok", [P, 3, D])
        raw = [sb(f"raw{s}", [P, UNIT]) for s in range(RING)]
        w_hi = [sb(f"w_hi{s}", [P, UNIT], F32R) for s in range(RING)]
        w_lo = [sb(f"w_lo{s}", [P, UNIT], F32R) for s in range(RING)]
        cst = sb("cst", [P, N_CONST])
        scores = sb("scores", [P, 2, SW])
        probs = sb("probs", [P, 4, PW])
        probs_t = sb("probs_t", [P, 2, PTW])
        q_aug = sb("q_aug", [P, 2, T])
        v_pair = sb("v_pair", [P, 2, 3, P])
        stats = sb("stats", [P, 2, 3, 3])
        sink_exp = sb("sink_exp", [P, 2, 3])
        rinv = sb("rinv", [P, 2, 3])
        y = sb("y", [P, 4, T])
        gated = sb("gated", [P, T])
        squares = sb("squares", [P, 2, T])
        total = sb("total", [P, T])
        rstd = sb("rstd", [P, T])
        eps = sb("eps", [P, 2])
        scales = sb("scales", [P, 2])
        ps = ctx.enter_context(nc.psum_tensor("ps", [P, 8, 512], F32))

        def c(name, rows=P):
            a, b = CONST[name]
            return cst[0:rows, a:b]

        ident, ones = c("ident"), c("ones")
        ln_par = c("ln").rearrange("p (n two k) -> p n two k", two=2, k=DC)
        conv_par = c("conv").rearrange("p (l j w) -> p l j w", l=DEPTH, w=4)
        gate_w = c("gate_w").rearrange("p (n k m) -> p n k m", n=2, k=DC)
        x_view = x.rearrange("k p t -> p k t")

        raw_landed = [sem(f"raw_landed{s}") for s in range(RING)]
        x_landed, const_landed, out_stored = sem("x_landed"), sem("const_landed"), sem("out_stored")
        hi_ready, lo_ready, w_used = sem("hi_ready"), sem("lo_ready"), sem("w_used")
        panel_done, bank_free = sem("panel_done"), sem("bank_free")
        init_done = sem("init_done")
        resid_added, mu_done, centered = sem("resid_added"), sem("mu_done"), sem("centered")
        squared, square_used, std_done = sem("squared"), sem("square_used"), sem("std_done")
        rescaled, norm_hi, affine_done = sem("rescaled"), sem("norm_hi"), sem("affine_done")
        h_ready = sem("h_ready")
        staged, scored, masked, negated = sem("staged"), sem("scored"), sem("masked"), sem("negated")
        exped, normed, transposed = sem("exped"), sem("normed"), sem("transposed")
        pt_copied, v_staged, mixed = sem("pt_copied"), sem("v_staged"), sem("mixed")
        o_hi, o_split = sem("o_hi"), sem("o_split")
        v_turned, v_copied = sem("v_turned"), sem("v_copied")
        ones_row, decay_moved = sem("ones_row"), sem("decay_moved")
        gate_done, gate_act, decay_done = sem("gate_done"), sem("gate_act"), sem("decay_done")
        swapped, roped = sem("swapped"), sem("roped")
        lat_sq, lat_sum, lat_std, lat_scaled, lat_hi, lat_ready = (
            sem(n) for n in ("lat_sq", "lat_sum", "lat_std", "lat_scaled", "lat_hi", "lat_ready"))
        conv_begun, silu_done, gate_mul, hid_hi_done, hid_ready = (
            sem(n) for n in ("conv_begun", "silu_done", "gate_mul", "hid_hi_done", "hid_ready"))
        dve_own, act_own, pool_own = sem("dve_own"), sem("act_own"), sem("pool_own")

        class Own:

            def __init__(self, eng, s):
                self.eng, self.s, self.base, self.k = eng, s, 0, 0
                self.i, self.per, self.looping = 0, 0, False

            def turn(self, i, per, first=0):
                if not self.looping:
                    self.base += self.k
                self.i, self.per, self.k, self.looping = i, per, 0, True
                self.off = self.base - first * per

            def turned(self, turns):
                assert self.k == self.per, (self.k, self.per)
                self.base += turns * self.per
                self.k, self.looping = 0, False

            def link(self, ins):
                ins.then_inc(self.s, 1)
                self.k += 1
                value = self.i * self.per + (self.off + self.k) if self.looping else self.base + self.k
                self.eng.wait_ge(self.s, value)

        def bank(p):
            return ps[:, p % BANKS, 0:T]

        def at(buf, i):
            return buf[:, i, :] if isinstance(i, int) else \
                buf[:, bass.ds(i, 1), :].rearrange("p o t -> p (o t)")

        def hidden(part, k):
            k, least = k if isinstance(k, tuple) else (k, k)
            if least < FA:
                return at((hid_hi, hid_lo)[part], k)
            return at(hid2[:, part], k - FA)

        def turns(eng, n, emit, first=0):
            if n - first == 1:
                emit(first)
            elif n > first:
                with eng.Fori(first, n) as i:
                    emit(i)

        block = ctx.enter_context(nc.Block())

        @block.sync
        def _(sp):
            sp.dma_start(h[:], x_view).then_inc(x_landed, 16)
            sp.dma_start(raw[0][:], weights[0]).then_inc(raw_landed[0], 16)
            sp.dma_start(cst[:], consts).then_inc(const_landed, 16)
            for u in range(1, RING):
                sp.dma_start(raw[u][:], weights[u]).then_inc(raw_landed[u], 16)

            def unit(u, s):
                sp.wait_ge(lo_ready, u - (RING - 1))
                src = weights[u] if isinstance(u, int) else weights[bass.ds(u, 1)].rearrange("a p n -> p (a n)")
                sp.dma_start(raw[s][:], src).then_inc(raw_landed[s], 16)

            full = N_UNITS // RING
            with sp.Fori(1, full) as i:
                for s in range(RING):
                    unit(i * RING + s, s)
            for u in range(full * RING, N_UNITS):
                unit(u, u % RING)

            for chunk in range(DC):
                sp.wait_ge(affine_done, 8 * (2 * DEPTH - 1) + chunk + 1)
                sp.dma_start(out[chunk], h[:, chunk, N_META:T]).then_inc(out_stored, 16)
            sp.wait_ge(out_stored, 16 * DC)

        @block.tensor
        def _(pe):
            def panel(s, u0, p0, i, j, rhs, ready=None):
                pn = i * s.body + (p0 + j)
                b = bank(p0 + j)
                if not (isinstance(pn, int) and pn < BANKS):
                    pe.wait_ge(bank_free, pn - (BANKS - 1))
                tiles = s.panels[j]
                new = set(s.new_units(j))
                for n, (u, t, k) in enumerate(tiles):
                    un = i * s.body_units + (u0 + u)
                    first = u in new
                    if first:
                        pe.wait_ge(lo_ready, un + 1)
                        new.discard(u)
                    if ready is not None and j == 0:
                        ready(k)
                    slot = (u0 + u) % RING
                    whi, wlo = w_hi[slot][:, t * P:(t + 1) * P], w_lo[slot][:, t * P:(t + 1) * P]
                    xhi, xlo = rhs(k)
                    m = pe.matmul(b, whi, xhi, start=n == 0, stop=False)
                    if first and not (isinstance(un, int) and un == 0):
                        m.then_inc(w_used, 1)
                    pe.matmul(b, whi, xlo, start=False, stop=False)
                    m = pe.matmul(b, wlo, xhi, start=False, stop=n == len(tiles) - 1)
                m.then_inc(panel_done, 1)

            def gemm(layer, name, rhs, ready=None, after=None, straight=False):
                s, u0, p0 = LAYERS[layer][name]

                def turn(i):
                    for j in range(s.body):
                        panel(s, u0, p0, i, j, rhs, ready)
                        if after is not None:
                            after(i, j)

                if straight:
                    for i in range(s.turns):
                        turn(i)
                else:
                    turns(pe, s.turns, turn)

            def from_h(k):
                return h_hi[:, k, :], h_lo[:, k, :]

            def from_first(k):
                return hid_hi[:, k, :], hid_lo[:, k, :]

            def from_latent(first):
                return lambda k: (hid_hi[:, LAT + first + k, :], hid_lo[:, LAT + first + k, :])

            def from_hidden(k):
                return hidden(0, k), hidden(1, k)

            def norm_ready(n):
                return lambda k: pe.wait_ge(h_ready, 8 * n + k + 1)

            n_v = [0]

            def turn_values(layer, n, stage):
                s, _, p0 = LAYERS[layer][stage]
                pe.wait_ge(bank_free, p0 + len(s.panels))
                for m in range(n):
                    b = ps[:, 4 + m % 2]
                    if m >= 2:
                        pe.wait_ge(v_copied, n_v[0] + m - 1)
                    for ch in (2, 0, 1):
                        a, e = ch * P, min(T, (ch + 1) * P)
                        t = pe.transpose(b[0:e - a, ch * P:(ch + 1) * P], q_all[:, m, a:e], ident)
                    t.then_inc(v_turned, 1)
                n_v[0] += n

            def attention(a, kind):
                rows = K_ROWS[kind]
                h0 = HEADS * a

                def step(i, j, scoring=True, turning=True, mixing=True):
                    hn = i * 4 + j
                    looping = not isinstance(hn, int)
                    if scoring:
                        s = j % 2
                        key = hn // 8 if kind == "swa" else hn
                        pe.wait_ge(staged, hn + (h0 + 1))
                        if looping or hn >= 4:
                            pe.wait_ge(masked, hn + (h0 - 3))
                        for ch, (lo, hi) in enumerate(CHUNKS):
                            if kind == "swa":
                                hi_q = max(hi, P)
                            else:
                                hi_q = hi
                            m = pe.matmul(ps[0:hi_q - lo, j, SCOL[ch]:SCOL[ch + 1]], q_aug[0:rows, s, lo:hi_q],
                                          at(keys, key)[0:rows, 0:hi], start=True, stop=True)
                        m.then_inc(scored, 1)
                    if turning:
                        s = (j - 3) % 2
                        pe.wait_ge(normed, hn + (h0 - 2))
                        if looping or hn >= 4:
                            pe.wait_ge(pt_copied, hn + (h0 - 3))
                        b, pr = ps[:, 4 + s], probs[:, (j - 3) % 4]

                        def turn(col, ch, key, keys_n=P):
                            q = CHUNKS[ch][1] - CHUNKS[ch][0]
                            c0 = PCOL[ch] + key
                            return pe.transpose(b[0:keys_n, col:col + q], pr[0:q, c0:c0 + keys_n], ident[0:q, 0:q])

                        turn(PT1 + TAIL - P, 1, P)
                        turn(PTW - P, 2, 2 * P, TAIL)
                        turn(0, 0, 0)
                        turn(N_META, 1, 0)
                        turn(N_META + P, 2, 0)
                        turn(PT1 + TAIL, 2, P).then_inc(transposed, 1)
                    if mixing:
                        s = (j - 4) % 2
                        pe.wait_ge(pt_copied, hn + (h0 - 3))
                        pe.wait_ge(v_staged, hn + (h0 - 3))
                        o = ps[:, 6 + ((j - 4) // 2) % 2]
                        pt = probs_t[:, s]
                        pe.matmul(o[:, 0:T], v_pair[:, s, 0], pt[:, 0:T], start=s == 0, stop=False)
                        pe.matmul(o[:, P:T], v_pair[:, s, 1], pt[:, PT1:PT2], start=False, stop=False)
                        pe.matmul(o[:, 2 * P:T], v_pair[0:TAIL, s, 2], pt[0:TAIL, PT2:PTW], start=False,
                                  stop=s == 1).then_inc(mixed, 1)

                for j in range(4):
                    step(0, j, turning=j >= 3, mixing=False)
                with pe.Fori(1, 4) as i:
                    for j in range(4):
                        step(i, j)
                for j in range(4):
                    step(4, j, scoring=False, turning=j < 3)

            def norm(n):
                pe.wait_ge(resid_added, 8 * n + 8)
                pe.matmul(ps[:, 5, 0:T], ones, total[:], start=True, stop=True).then_inc(mu_done, 1)
                for k in range(DC):
                    pe.wait_ge(squared, 8 * n + k + 1)
                    pe.matmul(ps[:, 6, 0:T], ones, squares[:, k % 2, :], start=k == 0,
                              stop=k == DC - 1).then_inc(square_used, 1)

            n_swap = [0]
            n_fox = 0
            pe.wait_ge(const_landed, 16)
            for a, kind in enumerate(KINDS):
                nr = norm_ready(2 * a)
                if kind == "fox":
                    gemm(a, "v", from_h, nr, straight=a == 0)
                    turn_values(a, 8, "v")
                    pe.wait_ge(v_copied, n_v[0])
                    gemm(a, "q", from_h)
                    for k in range(DC):
                        m = pe.matmul(ps[0:16, 6, 0:T], gate_w[:, n_fox, k, :], h[:, k, :],
                                      start=k == 0, stop=k == DC - 1)
                    m.then_inc(gate_done, 1)
                    gemm(a, "k", from_h)
                    pe.wait_ge(decay_moved, 16 * (n_fox + 1))
                    pe.wait_ge(ones_row, n_fox + 1)
                    n_fox += 1
                elif kind == "swa":
                    perm = c("perm_swa")
                    gemm(a, "v", from_h, nr)
                    turn_values(a, 1, "v")

                    def swap(src, done):
                        pe.wait_ge(bank_free, done)
                        pe.wait_ge(roped, n_swap[0])
                        pe.matmul(ps[:, 7, 0:T], perm, src, start=True, stop=True).then_inc(swapped, 1)
                        n_swap[0] += 1

                    gemm(a, "k", from_h)
                    swap(q_rope[:, 0, :], LAYERS[a]["k"][2] + 1)
                    base = n_swap[0]
                    pq = LAYERS[a]["q"][2]

                    def after(i, j):
                        pe.wait_ge(bank_free, i * 4 + (pq + j + 1))
                        pe.wait_ge(roped, i * 4 + (base + j))
                        pe.matmul(ps[:, 7, 0:T], perm, at(q_all, i * 4 + j),
                                  start=True, stop=True).then_inc(swapped, 1)

                    gemm(a, "q", from_h, after=after)
                    n_swap[0] += 8
                else:
                    perm = c("perm_mla")
                    gemm(a, "a", from_h, nr)
                    pe.wait_ge(bank_free, LAYERS[a]["a"][2] + 6)
                    pe.wait_ge(roped, n_swap[0])
                    pe.matmul(ps[:, 7, 0:T], perm, q_all[:, 5, :], start=True, stop=True).then_inc(swapped, 1)
                    n_swap[0] += 1
                    for k in range(5):
                        pe.wait_ge(lat_sq, k + 1)
                        pe.matmul(ps[:, 5 if k < 3 else 6, 0:T], ones, y[:, k % 4, :],
                                  start=k in (0, 3), stop=k in (2, 4)).then_inc(lat_sum, 1)
                    pe.wait_ge(lat_ready, 5)
                    gemm(a, "v", from_latent(3))
                    turn_values(a, 8, "v")
                    pe.wait_ge(v_copied, n_v[0])
                    gemm(a, "q", from_latent(0))
                    pr = LAYERS[a]["r"][2]
                    base = n_swap[0]

                    def after(i, j):
                        pe.wait_ge(bank_free, pr + j + 1)
                        pe.wait_ge(roped, base + j)
                        pe.matmul(ps[:, 7, 0:T], perm, q_rope[:, j, :], start=True, stop=True).then_inc(swapped, 1)

                    gemm(a, "r", from_latent(0), after=after)
                    n_swap[0] += 4
                    gemm(a, "k", from_latent(3))
                pe.wait_ge(v_copied, n_v[0])
                pe.wait_ge(bank_free, LAYERS[a]["o"][2])
                if ROPES[a]:
                    pe.wait_ge(roped, ROPES[a])
                attention(a, kind)
                pe.wait_ge(o_split, 8 * (a + 1))
                gemm(a, "o", from_first)
                norm(2 * a)
                gemm(a, "up", from_h, norm_ready(2 * a + 1))
                gemm(a, "down", from_hidden, ready=lambda k: pe.wait_ge(hid_ready, FC * a + k + 1),
                     straight=a == DEPTH - 1)
                norm(2 * a + 1)

        @block.scalar
        def _(act):
            own = Own(act, act_own)

            def split_hi(u):
                u, slot, rounds = u
                act.wait_ge(raw_landed[slot], rounds * 16)
                if not (isinstance(u, int) and u < RING):
                    act.wait_ge(w_used, u - (RING - 1))
                act.activation(w_hi[slot][:], raw[slot][:], ACT.Copy).then_inc(hi_ready, 1)

            def units_of(layer, name, i, j):
                s, u0, _ = LAYERS[layer][name]
                for u in s.new_units(j):
                    first = u0 + u + AHEAD
                    if isinstance(i, int) and i * s.body_units + first >= N_UNITS:
                        continue
                    yield (i * s.body_units + first, first % RING,
                           i * (s.body_units // RING) + (first // RING + 1)
                           if s.turns > 1 else first // RING + 1)

            def gemm(layer, name, evac=None, links=0, straight=False):
                s, _, p0 = LAYERS[layer][name]

                def turn(i):
                    own.turn(i, links)
                    for j in range(s.body):
                        for u in units_of(layer, name, i, j):
                            split_hi(u)
                        if evac is not None:
                            evac(i, j, i * s.body + (p0 + j))

                if straight:
                    for i in range(s.turns):
                        turn(i)
                else:
                    turns(act, s.turns, turn)
                own.turned(s.turns)

            n_v = [0]

            def copy_values(n):
                for m in range(n):
                    act.wait_ge(v_turned, n_v[0] + m + 1)
                    b = ps[:, 4 + m % 2]
                    act.activation(v_tok[0:16, 2, m * P:(m + 1) * P], b[0:16, 2 * P:3 * P], ACT.Copy)
                    act.activation(v_tok[:, 0:2, m * P:(m + 1) * P],
                                   b[:, 0:2 * P].rearrange("p (c n) -> p c n", c=2), ACT.Copy).then_inc(v_copied, 1)
                n_v[0] += n

            def attention(a, kind):
                h0 = HEADS * a

                def step(i, j, exping=True, copying=True, outputs=True):
                    hn = i * 4 + j
                    looping = not isinstance(hn, int)
                    if copying:
                        s = (j - 3) % 2
                        act.wait_ge(transposed, hn + (h0 - 2))
                        if looping or hn >= 5:
                            act.wait_ge(mixed, hn + (h0 - 4))
                        act.activation(probs_t[:, s, 0:PT2], ps[:, 4 + s, 0:PT2], ACT.Copy)
                        act.activation(probs_t[0:TAIL, s, PT2:PTW], ps[0:TAIL, 4 + s, PT2:PTW],
                                       ACT.Copy).then_inc(pt_copied, 1)
                    if exping:
                        s = j % 2
                        act.wait_ge(negated, hn + (h0 + 1))
                        if looping or hn >= 4:
                            act.wait_ge(transposed, hn + (h0 - 3))
                        if kind == "swa":
                            a0, _ = CONST["sinks"]
                            sk = cst[:, a0 + hn:a0 + hn + 1] if isinstance(hn, int) else cst[:, bass.ds(hn + a0, 1)]
                            act.activation(sink_exp[:, s, :], stats[:, s, 1, :], ACT.Exp, bias=sk)
                        for ch, (lo, hi) in enumerate(CHUNKS):
                            r = hi - lo
                            ins = act.activation(probs[0:r, j, PCOL[ch]:PCOL[ch] + hi],
                                                 scores[0:r, s, SCOL[ch]:SCOL[ch + 1]], ACT.Exp,
                                                 bias=stats[0:r, s, 1, ch:ch + 1],
                                                 accum_out=stats[0:r, s, 2, ch:ch + 1])
                        ins.then_inc(exped, 1)
                    if outputs and j % 2 == 1:
                        act.wait_ge(mixed, hn + (h0 - 3))
                        act.activation(at(hid_hi, i * 2 + (j - 5) // 2), ps[:, 6 + ((j - 5) // 2) % 2, 0:T],
                                       ACT.Copy).then_inc(o_hi, 1)

                for j in range(4):
                    step(0, j, copying=j >= 3, outputs=False)
                first = 1
                if a == 0:
                    for j in range(4):
                        step(1, j)
                    first = 2
                with act.Fori(first, 4) as i:
                    for j in range(4):
                        step(i, j)
                for j in range(4):
                    step(4, j, exping=False, copying=j < 3)

            def norm(n):
                for k in range(DC):
                    act.wait_ge(centered, 8 * n + k + 1)
                    if n or k >= 2:
                        act.wait_ge(square_used, 8 * n + k - 1)
                    act.activation(squares[:, k % 2, :], h[:, k, :], ACT.Square).then_inc(squared, 1)
                act.wait_ge(square_used, 8 * n + 8)
                act.activation(rstd[:], ps[:, 6, 0:T], ACT.Sqrt, bias=eps[:, 0:1]).then_inc(std_done, 1)
                last = n == 2 * DEPTH - 1
                for k in range(DC if not last else 0):
                    act.wait_ge(rescaled, 8 * n + k + 1)
                    act.activation(h_hi[:, k, :], h[:, k, :], ACT.Identity, scale=ln_par[:, n, 0, k:k + 1],
                                   bias=ln_par[:, n, 1, k:k + 1]).then_inc(norm_hi, 1)

            act.wait_ge(x_landed, 16)
            for k in range(DC):
                act.activation(h_hi[:, k, :], h[:, k, :], ACT.Copy).then_inc(norm_hi, 1)
            for u in range(AHEAD):
                split_hi((u, u, 1))
            act.wait_ge(const_landed, 16)
            act.wait_ge(init_done, 8)
            n_fox = 0
            for a, kind in enumerate(KINDS):
                if kind == "fox":
                    gemm(a, "v", straight=a == 0)
                    copy_values(8)
                    gemm(a, "q")
                    z, mag, e, u1, lnu = (y[0:16, 0, :], y[0:16, 1, :], y[0:16, 2, :], y[0:16, 3, :], gated[0:16, :])
                    act.wait_ge(gate_done, n_fox + 1)
                    gb = CONST["gate_b"][0] + n_fox
                    bias = cst[0:16, gb:gb + 1]
                    act.activation(z, ps[0:16, 6, 0:T], ACT.Identity, bias=bias)
                    own.link(act.activation(mag, ps[0:16, 6, 0:T], ACT.Abs, bias=bias))
                    own.link(act.activation(e, mag, ACT.Exp, scale=-1.0))
                    own.link(act.activation(u1, e, ACT.Identity, bias=1.0))
                    act.activation(lnu, u1, ACT.Ln).then_inc(gate_act, 1)
                    gemm(a, "k")
                    n_fox += 1
                elif kind == "swa":
                    gemm(a, "v")
                    copy_values(1)
                    gemm(a, "k")
                    gemm(a, "q")
                else:
                    gemm(a, "a")
                    pa = LAYERS[a]["a"][2]
                    act.wait_ge(bank_free, pa + 5)
                    for k in range(5):
                        if k >= 4:
                            act.wait_ge(lat_sum, k - 3)
                        act.activation(y[:, k % 4, :], q_all[:, k, :], ACT.Square).then_inc(lat_sq, 1)
                    for k, (width, at_sum) in enumerate(((Q_LORA, 3), (KV_LORA, 5))):
                        act.wait_ge(lat_sum, at_sum)
                        act.activation(squares[:, k, :], ps[:, 5 + k, 0:T], ACT.Sqrt, scale=float(D) / width,
                                       bias=eps[:, 1:2]).then_inc(lat_std, 1)
                    g0 = CONST["rms_g"][0]
                    for k in range(5):
                        act.wait_ge(lat_scaled, k + 1)
                        act.activation(hid_hi[:, LAT + k, :], q_all[:, k, :], ACT.Identity,
                                       scale=cst[:, g0 + k:g0 + k + 1]).then_inc(lat_hi, 1)
                    gemm(a, "v")
                    copy_values(8)
                    gemm(a, "q")
                    gemm(a, "r")
                    gemm(a, "k")
                attention(a, kind)
                gemm(a, "o")
                norm(2 * a)

                pu = LAYERS[a]["up"][2]

                def silu(k, slot):
                    act.wait_ge(bank_free, k * 2 + (pu + 1 - 2 * FC * a))
                    act.activation(y[:, 2 * slot, :], y[:, 2 * slot, :], ACT.Silu).then_inc(silu_done, 1)

                def hidden_hi(k, dst):
                    act.wait_ge(gate_mul, k + 1)
                    act.activation(dst, gated[:], ACT.Copy).then_inc(hid_hi_done, 1)

                def up_turn(least):
                    def turn(i):
                        for j in range(4):
                            if least or j >= 2:
                                k = i * 2 + (FC * a + j // 2 - 1)
                                if j % 2 == 0:
                                    silu(k, (j // 2 + 1) % 2)
                                else:
                                    hidden_hi(k, hidden(0, (i * 2 + (j // 2 - 1), least + j // 2 - 1)))
                            for u in units_of(a, "up", i, j):
                                split_hi(u)
                            idx = i * 4 + j
                            par = conv_par[:, a]
                            col = (lambda w: par[:, idx, w:w + 1]) if isinstance(idx, int) else \
                                (lambda w: par[:, bass.ds(idx, 1), w])
                            act.wait_ge(panel_done, i * 4 + (pu + j + 1))
                            act.activation(y[:, j, :], bank(pu + j), ACT.Identity,
                                           scale=col(2), bias=col(3)).then_inc(conv_begun, 1)
                    return turn

                turns(act, 1, up_turn(0))
                turns(act, SPLIT, up_turn(2), first=1)
                turns(act, FC // 2, up_turn(2 * SPLIT), first=SPLIT)
                silu(FC * a + FC - 1, 1)
                hidden_hi(FC * a + FC - 1, hidden(0, FC - 1))
                gemm(a, "down", straight=a == DEPTH - 1)
                norm(2 * a + 1)

        @block.gpsimd
        def _(pool):
            own = Own(pool, pool_own)
            pool.memset(eps[:, 0:1], LN_EPS).then_inc(init_done, 1)
            pool.memset(eps[:, 1:2], RMS_EPS).then_inc(init_done, 1)
            pool.memset(scales[:, 0:1], SCALE["fox"]).then_inc(init_done, 1)
            pool.memset(scales[:, 1:2], SCALE["mla"]).then_inc(init_done, 1)
            for buf, value in ((stats, 1.0), (v_tok, 0.0), (probs, 0.0), (v_pair, 0.0)):
                pool.memset(buf[:], value).then_inc(init_done, 1)

            def norm(n, stage):
                _, _, p0 = LAYERS[n // 2][stage]
                if n:
                    pool.wait_ge(mu_done, n)
                own.link(pool.memset(total[:], 0.0))
                for k in range(DC):
                    pool.wait_ge(bank_free, p0 + k + 1)
                    pool.tensor_tensor(total[:], total[:], h[:, k, :], ALU.add).then_inc(resid_added, 1)
                    pool.wait_ge(resid_added, 8 * n + k + 1)
                last = n == 2 * DEPTH - 1
                for k in range(DC):
                    if last:
                        pool.wait_ge(rescaled, 8 * n + k + 1)
                    else:
                        pool.wait_ge(norm_hi, 8 * (n + 1) + k + 1)
                    pool.tensor_scalar(h[:, k, :], h[:, k, :], ln_par[:, n, 0, k:k + 1],
                                       ln_par[:, n, 1, k:k + 1], ALU.mult, ALU.add).then_inc(affine_done, 1)

            def attention(a, kind):
                h0 = HEADS * a
                n = 1 if kind == "mla" else 0
                scale = scales[:, n:n + 1].broadcast_to([P, T])

                def step(i, j, queries=True, values=True):
                    hn = i * 4 + j
                    looping = not isinstance(hn, int)
                    if queries:
                        s = j % 2
                        if looping or hn >= 2:
                            pool.wait_ge(scored, hn + (h0 - 1))
                        if looping or hn >= 5:
                            pool.wait_ge(v_staged, hn + (h0 - 4))
                        r = 64 * (j % 2)
                        src = at(q_all, i * 2 + j // 2)[r:r + 64]
                        ins = pool.tensor_tensor(q_aug[0:64, s, :], src, scale[r:r + 64], ALU.mult)
                        if kind == "mla":
                            src = at(q_rope, i)[32 * j:32 * j + 32]
                            own.link(ins)
                            ins = pool.tensor_tensor(q_aug[64:96, s, :], src, scale[32 * j:32 * j + 32], ALU.mult)
                        ins.then_inc(staged, 1)
                        pool.wait_ge(staged, hn + (h0 + 1))
                    if values:
                        s = j % 2
                        if looping or hn >= 6:
                            pool.wait_ge(mixed, hn + (h0 - 5))
                        col = ((hn - 4) // 8 if kind == "swa" else hn - 4) * HD
                        src = v_tok[:, :, col:col + HD] if isinstance(col, int) else v_tok[:, :, bass.ds(col, HD)]
                        pool.tensor_copy(v_pair[:, s, :, s * HD:(s + 1) * HD], src).then_inc(v_staged, 1)

                for j in range(4):
                    step(0, j, values=False)
                first = 1
                if a == 0:
                    for j in range(4):
                        step(1, j)
                    first = 2
                with pool.Fori(first, 4) as i:
                    own.turn(i, 4 if kind == "mla" else 0, first=first)
                    for j in range(4):
                        step(i, j)
                own.turned(4 - first)
                for j in range(4):
                    step(4, j, queries=False)

            n_fox = 0
            n_v = 0
            pool.wait_ge(init_done, 8)
            pool.wait_ge(const_landed, 16)
            for a, kind in enumerate(KINDS):
                if kind == "fox":
                    pool.wait_ge(decay_done, n_fox + 1)
                    pool.dma_start(keys[64:65, :, :], y[0:16, 1, :]).then_inc(decay_moved, 16)
                    pool.wait_ge(decay_moved, 16 * (n_fox + 1))
                    n_fox += 1
                n_v += 1 if kind == "swa" else DC
                pool.wait_ge(bank_free, LAYERS[a]["o"][2])
                pool.wait_ge(v_copied, n_v)
                if ROPES[a]:
                    pool.wait_ge(roped, ROPES[a])
                attention(a, kind)
                norm(2 * a, "o")
                pu = LAYERS[a]["up"][2]

                def gate(k, slot, hi, lo):
                    pool.wait_ge(bank_free, k * 2 + (pu + 2 - 2 * FC * a))
                    pool.wait_ge(silu_done, k + 1)
                    if not (isinstance(k, int) and k == 0):
                        pool.wait_ge(hid_ready, k)
                    pool.tensor_tensor(gated[:], y[:, 2 * slot, :], y[:, 2 * slot + 1, :],
                                       ALU.mult).then_inc(gate_mul, 1)
                    pool.wait_ge(hid_hi_done, k + 1)
                    pool.tensor_tensor(lo, gated[:], hi.bitcast(F32), ALU.subtract).then_inc(hid_ready, 1)

                def gate_turn(least):
                    def turn(i):
                        for n in range(2):
                            if least or n:
                                k = (i * 2 + (n - 1), least + n - 1)
                                gate(i * 2 + (FC * a + n - 1), (n + 1) % 2, hidden(0, k), hidden(1, k))
                    return turn

                turns(pool, 1, gate_turn(0))
                turns(pool, SPLIT, gate_turn(2), first=1)
                turns(pool, FC // 2, gate_turn(2 * SPLIT), first=SPLIT)
                gate(FC * a + FC - 1, 1, hidden(0, FC - 1), hidden(1, FC - 1))
                norm(2 * a + 1, "down")

        @block.vector
        def _(dve):
            own = Own(dve, dve_own)
            copy = dve.tensor_copy

            def tt(out_, a_, b_, op):
                return dve.tensor_tensor(out_, a_, b_, op)

            def split_lo(u, slot):
                dve.wait_ge(hi_ready, u + 1)
                tt(w_lo[slot][:], raw[slot][:], w_hi[slot][:].bitcast(F32), ALU.subtract).then_inc(lo_ready, 1)

            def split_units(layer, name, i, j):
                s, u0, _ = LAYERS[layer][name]
                for u in s.new_units(j):
                    first = u0 + u + AHEAD
                    if isinstance(i, int) and i * s.body_units + first >= N_UNITS:
                        continue
                    split_lo(i * s.body_units + first, first % RING)

            def gemm(layer, name, evac, links=0, straight=False):
                s, _, p0 = LAYERS[layer][name]

                def turn(i):
                    own.turn(i, links)
                    for j in range(s.body):
                        split_units(layer, name, i, j)
                        dve.wait_ge(panel_done, i * s.body + (p0 + j + 1))
                        evac(i, j, bank(p0 + j), i * s.body + (p0 + j))

                if straight:
                    for i in range(s.turns):
                        turn(i)
                else:
                    turns(dve, s.turns, turn)
                own.turned(s.turns)

            def to_q(body):
                def evac(i, j, b, pn):
                    copy(at(q_all, i * body + j), b).then_inc(bank_free, 1)
                return evac

            def to_keys(body):
                def evac(i, j, b, pn):
                    m2 = i * (2 * body) + 2 * j
                    copy(keys_at(m2), b[0:64])
                    copy(keys_at(m2 + 1), b[64:128]).then_inc(bank_free, 1)
                return evac

            def keys_at(n):
                return at(keys, n)[0:64]

            def rope(qn, swap_no, cos, sin, dst, rows=P):
                tt(y[0:rows, 0, :], qn[0:rows], cos[0:rows], ALU.mult)
                dve.wait_ge(swapped, swap_no)
                own.link(tt(y[0:rows, 1, :], ps[0:rows, 7, 0:T], sin[0:rows], ALU.mult))
                return tt(dst, y[0:rows, 0, :], y[0:rows, 1, :], ALU.add)

            def attention(a, kind):
                h0, p0 = HEADS * a, HEADS // 2 * a
                mask = c("mask_window" if kind == "swa" else "mask_causal")

                def step(i, j, masking=True, norming=True, splitting=True):
                    hn = i * 4 + j
                    looping = not isinstance(hn, int)
                    if masking:
                        s = j % 2
                        dve.wait_ge(scored, hn + (h0 + 1))
                        dve.memset(stats[:, s, 2, :], 1.0)
                        for ch, (lo, hi) in enumerate(CHUNKS):
                            r, cols = hi - lo, slice(SCOL[ch], SCOL[ch + 1])
                            ins = dve.tensor_tensor_reduce(
                                out=scores[0:r, s, cols], in0=ps[0:r, j, cols],
                                in1=mask[0:r, cols], scale=1.0, scalar=-3.0e38, op0=ALU.add, op1=ALU.max,
                                accum_out=stats[0:r, s, 0, ch:ch + 1])
                        ins.then_inc(masked, 1)
                        dve.wait_ge(masked, hn + (h0 + 1))
                        if kind == "swa":
                            a0, _ = CONST["sinks"]
                            sk = cst[:, a0 + hn:a0 + hn + 1] if isinstance(hn, int) else cst[:, bass.ds(hn + a0, 1)]
                            dve.tensor_scalar(stats[:, s, 1, :], stats[:, s, 0, :], sk, -1.0,
                                              ALU.max, ALU.mult).then_inc(negated, 1)
                        else:
                            dve.tensor_scalar(stats[:, s, 1, :], stats[:, s, 0, :], -1.0, None,
                                              ALU.mult).then_inc(negated, 1)
                    if norming:
                        s = (j - 1) % 2
                        dve.wait_ge(exped, hn + h0)
                        if kind == "swa":
                            own.link(tt(stats[:, s, 2, :], stats[:, s, 2, :], sink_exp[:, s, :], ALU.add))
                        own.link(dve.reciprocal(rinv[:, s, :], stats[:, s, 2, :]))
                        for ch, (lo, hi) in enumerate(CHUNKS):
                            pr = probs[0:hi - lo, (j - 1) % 4, PCOL[ch]:PCOL[ch] + hi]
                            ins = dve.tensor_scalar(pr, pr, rinv[0:hi - lo, s, ch:ch + 1], None, ALU.mult)
                        ins.then_inc(normed, 1)
                    if splitting and j % 2 == 1:
                        pair = i * 2 + (j - 5) // 2
                        dve.wait_ge(o_hi, pair + (p0 + 1))
                        tt(at(hid_lo, pair), ps[:, 6 + ((j - 5) // 2) % 2, 0:T],
                           at(hid_hi, pair).bitcast(F32), ALU.subtract).then_inc(o_split, 1)

                for j in range(4):
                    step(0, j, norming=j >= 1, splitting=False)
                with dve.Fori(1, 4) as i:
                    own.turn(i, 8 if kind == "swa" else 4, first=1)
                    for j in range(4):
                        step(i, j)
                own.turned(3)
                for j in range(4):
                    step(4, j, masking=False, norming=j < 1)

            def residual(i, j, b, pn, body=4):
                hk = at(h, i * body + j)
                dve.scalar_tensor_tensor(hk, hk, ALPHA, b, ALU.mult, ALU.add).then_inc(bank_free, 1)

            def norm(n):
                last = n == 2 * DEPTH - 1
                dve.wait_ge(mu_done, n + 1)
                for k in range(DC):
                    tt(h[:, k, :], h[:, k, :], ps[:, 5, 0:T], ALU.subtract).then_inc(centered, 1)
                dve.wait_ge(std_done, n + 1)
                own.link(dve.reciprocal(rstd[:], rstd[:]))

                def lo_part(k):
                    dve.wait_ge(affine_done, 8 * n + k + 1)
                    tt(h_lo[:, k, :], h[:, k, :], h_hi[:, k, :].bitcast(F32), ALU.subtract).then_inc(h_ready, 1)

                for k in range(DC):
                    dve.wait_ge(squared, 8 * n + k + 1)
                    tt(h[:, k, :], h[:, k, :], rstd[:], ALU.mult).then_inc(rescaled, 1)
                    if k >= 3 and not last:
                        lo_part(k - 3)
                if not last:
                    for k in range(DC - 3, DC):
                        lo_part(k)

            for k in range(DC):
                dve.wait_ge(norm_hi, k + 1)
                tt(h_lo[:, k, :], h[:, k, :], h_hi[:, k, :].bitcast(F32), ALU.subtract).then_inc(h_ready, 1)
            for u in range(AHEAD):
                split_lo(u, u)
            dve.wait_ge(const_landed, 16)
            dve.wait_ge(init_done, 8)
            n_fox, n_swap, n_v = 0, 0, 0
            for a, kind in enumerate(KINDS):
                if kind == "fox":
                    if a:
                        dve.wait_ge(scored, HEADS * a)
                    dve.memset(q_aug[64:65, :, 0:T], 1.0).then_inc(ones_row, 1)
                    gemm(a, "v", to_q(4))
                    n_v += 8
                    dve.wait_ge(v_turned, n_v)
                    gemm(a, "q", to_q(4))
                    z, mag, e, u1, lnu = (y[0:16, 0, :], y[0:16, 1, :], y[0:16, 2, :], y[0:16, 3, :], gated[0:16, :])
                    zero = squares[0:16, 0, :]
                    dve.wait_ge(gate_act, n_fox + 1)
                    own.link(dve.tensor_scalar(u1, u1, -1.0, None, ALU.add))
                    own.link(dve.tensor_scalar(zero, u1, 0.0, None, ALU.is_equal))
                    tt(lnu, lnu, zero, ALU.add)
                    own.link(tt(u1, u1, zero, ALU.add))
                    own.link(dve.reciprocal(u1, u1))
                    own.link(tt(lnu, lnu, u1, ALU.mult))
                    own.link(tt(lnu, lnu, e, ALU.mult))
                    own.link(dve.tensor_scalar(z, z, -1.0, 0.0, ALU.mult, ALU.max))
                    own.link(tt(lnu, lnu, z, ALU.add))
                    own.link(dve.tensor_scalar(zero, zero, 0.0, 1.0, ALU.mult, ALU.add))
                    dve.tensor_tensor_scan(mag, zero, lnu, 0.0, ALU.mult, ALU.add).then_inc(decay_done, 1)
                    gemm(a, "k", to_keys(4))
                    n_fox += 1
                elif kind == "swa":
                    cos, sin = c("cos_swa"), c("sin_swa")
                    gemm(a, "v", to_q(1))
                    n_v += 1

                    def k_evac(i, j, b, pn):
                        copy(q_rope[:, 0, :], b).then_inc(bank_free, 1)
                        dve.wait_ge(bank_free, pn + 1)

                    gemm(a, "k", k_evac)
                    n_swap += 1
                    own.link(rope(q_rope[:, 0, :], n_swap, cos, sin, q_rope[:, 0, :]))
                    copy(keys[0:64, 0, :], q_rope[0:64, 0, :])
                    copy(keys[0:64, 1, :], q_rope[64:128, 0, :]).then_inc(roped, 1)
                    dve.wait_ge(v_turned, n_v)
                    base = n_swap

                    def q_evac(i, j, b, pn):
                        qn = at(q_all, i * 4 + j)
                        copy(qn, b).then_inc(bank_free, 1)
                        dve.wait_ge(bank_free, pn + 1)
                        if isinstance(i, int):
                            dve.wait_ge(roped, base + i * 4 + j)
                        else:
                            dve.wait_ge(roped, i * 4 + (base + j))
                        rope(qn, i * 4 + (base + j + 1), cos, sin, qn).then_inc(roped, 1)

                    gemm(a, "q", q_evac, links=4)
                    n_swap += 8
                else:
                    cos, sin = c("cos_mla"), c("sin_mla")
                    gemm(a, "a", to_q(6))
                    n_swap += 1
                    pa = LAYERS[a]["a"][2]
                    dve.wait_ge(bank_free, pa + 6)
                    own.link(tt(scores[0:32, 0, 0:T], q_all[0:32, 5, :], cos[0:32], ALU.mult))
                    dve.wait_ge(swapped, n_swap)
                    own.link(tt(scores[0:32, 1, 0:T], ps[0:32, 7, 0:T], sin[0:32], ALU.mult))
                    own.link(tt(scores[0:32, 0, 0:T], scores[0:32, 0, 0:T], scores[0:32, 1, 0:T], ALU.add))
                    copy(keys[64:96, :, :], scores[0:32, 0, 0:T].unsqueeze(1).broadcast_to([32, HEADS, T])).then_inc(roped, 1)
                    g0 = CONST["rms_g"][0]
                    for k in range(5):
                        buf = squares[:, k // 3, :]
                        if k in (0, 3):
                            dve.wait_ge(lat_std, 1 + k // 3)
                            own.link(dve.reciprocal(buf, buf))
                        dve.wait_ge(lat_sq, k + 1)
                        tt(q_all[:, k, :], q_all[:, k, :], buf, ALU.mult).then_inc(lat_scaled, 1)
                        dve.wait_ge(lat_hi, k + 1)
                        dve.scalar_tensor_tensor(hid_lo[:, LAT + k, :], q_all[:, k, :], cst[:, g0 + k:g0 + k + 1],
                                                 hid_hi[:, LAT + k, :].bitcast(F32), ALU.mult,
                                                 ALU.subtract).then_inc(lat_ready, 1)
                    gemm(a, "v", to_q(8))
                    n_v += 8
                    dve.wait_ge(v_turned, n_v)
                    gemm(a, "q", to_q(8))
                    base = n_swap

                    def r_evac(i, j, b, pn):
                        qn = q_rope[:, j, :]
                        copy(qn, b).then_inc(bank_free, 1)
                        dve.wait_ge(bank_free, pn + 1)
                        dve.wait_ge(roped, base + j)
                        rope(qn, base + j + 1, cos, sin, qn).then_inc(roped, 1)

                    gemm(a, "r", r_evac, links=4)
                    n_swap += 4
                    gemm(a, "k", to_keys(8))
                attention(a, kind)
                gemm(a, "o", residual)
                norm(2 * a)

                def conv(i, j, b, pn):
                    idx = i * 4 + j
                    par = conv_par[:, a]
                    col = (lambda w: par[:, idx, w:w + 1]) if isinstance(idx, int) else \
                        (lambda w: par[:, bass.ds(idx, 1), w])
                    yj = y[:, j, :]
                    dve.wait_ge(conv_begun, i * 4 + (2 * FC * a + j + 1))
                    own.link(dve.scalar_tensor_tensor(yj[:, 1:T], b[:, 0:T - 1], col(1), yj[:, 1:T],
                                                      ALU.mult, ALU.add))
                    dve.scalar_tensor_tensor(yj[:, 2:T], b[:, 0:T - 2], col(0), yj[:, 2:T],
                                             ALU.mult, ALU.add).then_inc(bank_free, 1)

                gemm(a, "up", conv, links=4)
                gemm(a, "down", residual, straight=a == DEPTH - 1)
                norm(2 * a + 1)



def panels(w):
    k, n = w.shape
    return w.reshape(k // P, P, n // P, P).transpose(2, 1, 0, 3)


def units(w, per_unit=1):
    a = panels(w)
    n, _, kt, _ = a.shape
    a = a.reshape(n // per_unit, per_unit, P, kt, P).transpose(0, 2, 1, 3, 4).reshape(n // per_unit, P, -1)
    full = np.zeros((a.shape[0], P, UNIT), a.dtype)
    full[:, :, :a.shape[2]] = a
    return full


def down_units(w):
    a = panels(w)
    full = np.zeros((DC, 3, P, UNIT), w.dtype)
    k = 0
    for u, n in enumerate(DOWN_TILES):
        full[:, u, :, :n * P] = a[:, :, k:k + n].reshape(DC, P, n * P)
        k += n
    return full.reshape(3 * DC, P, UNIT)


def layer_units(a, kind, inp):
    j = a // 3
    if kind == "fox":
        w = inp["fox_w_in"][j]
        mixer = [w[:, 2 * D:3 * D], w[:, :D], w[:, D:2 * D], inp["fox_w_o"][j]]
        mixer = [units(m) for m in mixer]
    elif kind == "swa":
        w = inp["swa_w_in"][j]
        kd = 2 * HD
        mixer = [units(m) for m in (w[:, D + kd:], w[:, D:D + kd], w[:, :D], inp["swa_w_o"][j])]
    else:
        wa = inp["mla_w_a"][j]
        wide = np.zeros((D, 6 * P), wa.dtype)
        wide[:, :wa.shape[1]] = wa
        uq = inp["mla_w_uq"][j].reshape(Q_LORA, HEADS, HD + MLA_ROPE)
        ukv = inp["mla_w_ukv"][j].reshape(KV_LORA, HEADS, 2 * HD)
        mixer = [units(wide), units(ukv[:, :, HD:].reshape(KV_LORA, D), 4),
                 units(uq[:, :, :HD].reshape(Q_LORA, D), 2),
                 units(uq[:, :, HD:].reshape(Q_LORA, HEADS * MLA_ROPE), 2),
                 units(ukv[:, :, :HD].reshape(KV_LORA, D), 4), units(inp["mla_w_o"][j])]
    up = units(inp["ffn_w_in"][a])
    up = np.stack([up[:FC], up[FC:]], 1).reshape(2 * FC, P, UNIT)
    return mixer + [up, down_units(inp["ffn_w_out"][a])]


def rope_tables(dim, theta, period):
    inv = (np.float32(theta) ** (-np.arange(0, dim, 2, dtype=np.float32) / np.float32(dim))).astype(np.float32)
    ang = np.arange(T, dtype=np.float32)[:, None] * inv[None, :]
    cos, sin = np.ones((P, T), np.float32), np.zeros((P, T), np.float32)
    perm = np.zeros((P, P), np.float32)
    half = dim // 2
    for p in range(P):
        d = p % period
        if d < dim:
            cos[p] = np.cos(ang[:, d % half])
            sin[p] = np.sin(ang[:, d % half]) * (-1 if d < half else 1)
            perm[p + half if d < half else p - half, p] = 1.0
    return cos, sin, perm


def masks():
    both = []
    for window in (T, WINDOW):
        m = np.full((P, SW), NEG, np.float32)
        for ch, (lo, hi) in enumerate(CHUNKS):
            q, k = np.arange(lo, hi)[:, None], np.arange(hi)[None, :]
            seen = (k <= q) & ((q - k < window) | (k < N_META))
            m[:hi - lo, SCOL[ch]:SCOL[ch + 1]] = np.where(seen, 0.0, NEG)
        both.append(m)
    return both


def const_block(inp):
    block = np.zeros((P, N_CONST), np.float32)

    def put(name, a, rows=P):
        lo, hi = CONST[name]
        block[:rows, lo:hi] = a.reshape(rows, hi - lo)

    put("ident", np.eye(P, dtype=np.float32))
    put("ones", np.full((P, P), 1.0 / D, np.float32))
    for name, args in (("swa", (ROPE_DIM, 500000.0, HD)), ("mla", (MLA_ROPE, 10000.0, MLA_ROPE))):
        cos, sin, perm = rope_tables(*args)
        put("cos_" + name, cos)
        put("sin_" + name, sin)
        put("perm_" + name, perm)
    causal, window = masks()
    put("mask_causal", causal)
    put("mask_window", window)
    ln = np.stack([np.stack([inp["ln1_g"], inp["ln1_b"]], 1), np.stack([inp["ln2_g"], inp["ln2_b"]], 1)], 1)
    put("ln", ln.reshape(DEPTH * 4, DC, P).transpose(2, 0, 1))
    cv = np.concatenate([inp["ffn_conv_w"], inp["ffn_conv_b"][:, None]], 1)
    put("conv", cv.reshape(DEPTH, 4, 2, FC, P).transpose(4, 0, 3, 2, 1))
    put("sinks", np.broadcast_to(inp["swa_sinks"][0], (P, HEADS)))
    put("gate_b", inp["fox_b_f"].T, HEADS)
    put("gate_w", inp["fox_w_in"][:, :, 3 * D:].reshape(2, DC, P, HEADS).transpose(2, 0, 1, 3))
    g = np.concatenate([inp["mla_g_q"][0], inp["mla_g_kv"][0]])
    put("rms_g", g.reshape(5, P).T)
    return block


def kernel(**inputs):
    import concourse.bacc as bacc
    from concourse.bass_utils import run_bass_kernel_spmd

    inp = {k: np.asarray(v) for k, v in inputs.items()}
    tokens = np.concatenate([inp["meta_tokens"], inp["x"][0]], 0)
    arrays = {
        "in_x": np.ascontiguousarray(tokens.T.reshape(DC, P, T)),
        "in_weights": np.concatenate([u for a, kind in enumerate(KINDS) for u in layer_units(a, kind, inp)], 0),
        "in_consts": const_block(inp),
    }
    assert arrays["in_weights"].shape[0] == N_UNITS
    nc = bacc.Bacc("TRN2", target_bir_lowering=False, num_devices=1)
    args = [nc.dram_tensor(n, a.shape, mybir.dt.from_np(a.dtype), kind="ExternalInput").ap()
            for n, a in arrays.items()]
    out = nc.dram_tensor("out_0", (DC, P, SEQ), F32, kind="ExternalOutput").ap()
    build_program(nc, *args, out)
    got = run_bass_kernel_spmd(nc, [arrays], core_ids=[0]).results[0]["out_0"]
    return np.ascontiguousarray(got.reshape(D, SEQ).T)[None]
```

```python
from contextlib import ExitStack

import numpy as np

import concourse.bass as bass
from concourse import mybir

F32 = mybir.dt.float32
F32R = mybir.dt.float32r
ALU = mybir.AluOpType
ACT = mybir.ActivationFunctionType

P = 128
D = 1024
DC = D // P
SEQ = 256
N_META = 16
T = SEQ + N_META
DEPTH = 4
ALPHA = (2.0 * DEPTH) ** 0.25
LN_EPS = 1e-5
RMS_EPS = 1e-6
NEG = -1e30
HEADS = 16
HD = 64
ROPE_DIM = HD // 4
WINDOW = 128
Q_LORA, KV_LORA, MLA_ROPE = 384, 256, 32
D_FF = 2816
FC = D_FF // P
FA = 13
SPLIT = (FA + 1) // 2
LAT = 8
UNIT = 8 * P
RING = 4
CENTER_DVE = 5
AHEAD = RING - 1
BANKS = 4
X_PARTS = 2

CHUNKS = ((0, N_META), (N_META, N_META + P), (N_META + P, T))
SCOL = (0, 16, 160, 432)
SW = SCOL[3]
PCOL = (0, P, 3 * P)
PW = PCOL[2] + T
TAIL = T - 2 * P
PT1, PT2, PTW = T, T + P + TAIL, T + P + 2 * TAIL

KINDS = tuple(("fox", "swa", "mla")[i % 3] for i in range(DEPTH))
K_ROWS = {"fox": HD + 1, "swa": HD, "mla": HD + MLA_ROPE}
SCALE = {"fox": HD ** -0.5, "swa": HD ** -0.5, "mla": (HD + MLA_ROPE) ** -0.5}


class Stage:

    def __init__(self, name, panels, units, body=None):
        self.name, self.panels, self.units = name, panels, units
        self.body = body or len(panels)
        self.turns = len(panels) // self.body
        self.body_units = units // self.turns

    def new_units(self, j):
        before = {u for p in self.panels[:j] for u, _, _ in p}
        return sorted({u for u, _, _ in self.panels[j]} - before)


def whole(name, n, body=None):
    return Stage(name, [[(j, k, k) for k in range(DC)] for j in range(n)], n, body)


def parts(name, n, kt, per_unit):
    return Stage(name, [[(j // per_unit, (j % per_unit) * kt + k, k) for k in range(kt)]
                        for j in range(n)], n // per_unit)


DOWN_TILES = (8, 7, 7)


def down(name):
    one = [(u, t, sum(DOWN_TILES[:u]) + t) for u in range(3) for t in range(DOWN_TILES[u])]
    return Stage(name, [[(3 * j + u, t, k) for u, t, k in one] for j in range(DC)], 3 * DC, 4)


MIXER = {
    "fox": [whole("v", 8, 4), whole("q", 8, 4), whole("k", 8, 4), whole("o", 8, 4)],
    "swa": [whole("vk", 2), whole("q", 8, 4), whole("o", 8, 4)],
    "mla": [whole("a", 6), parts("q", 8, 3, 2), parts("r", 4, 3, 2), parts("v", 8, 2, 4),
            parts("k", 8, 2, 4), whole("o", 8, 4)],
}
FFN = [whole("up", 2 * FC, 4), down("down")]


def plan():
    u = p = 0
    layers = []
    for kind in KINDS:
        stages = {}
        for s in MIXER[kind] + FFN:
            stages[s.name] = (s, u, p)
            u += s.units
            p += len(s.panels)
        layers.append(stages)
    return layers, u, p


LAYERS, N_UNITS, _ = plan()
NEXT = [s for a, kind in enumerate(KINDS) for s in
        ("up", MIXER[KINDS[a + 1]][0].name if a + 1 < DEPTH else None)]
LAST_FROM = {"o": N_META - 2, "up": N_META - 2, "down": N_META}
WARM = 40
ROPES = [sum({"fox": 0, "swa": 1 + 8, "mla": 1 + 4}[k] for k in KINDS[:a + 1]) for a in range(DEPTH)]


def const_columns():
    at, n = {}, 0
    for name, width in (
        ("ident", P), ("ones", P), ("perm_swa", P), ("perm_mla", P),
        ("mask_causal", SW), ("mask_window", SW),
        ("cos_swa", T), ("sin_swa", T), ("cos_mla", T), ("sin_mla", T),
        ("ln", DEPTH * 2 * 2 * DC), ("conv", DEPTH * 2 * FC * 4), ("sinks", HEADS),
        ("gate_b", 2), ("gate_w", 2 * DC * 16), ("rms_g", 5),
    ):
        at[name] = (n, n + width)
        n += width
    return at, n


CONST, N_CONST = const_columns()


def build_program(nc, x, weights, consts, out):
    with ExitStack() as ctx:
        def sb(name, shape, dt=F32):
            return ctx.enter_context(nc.sbuf_tensor(name, shape, dt))

        def sem(name):
            return ctx.enter_context(nc.semaphore(name))

        h = sb("h", [P, DC, T])
        h_hi = sb("h_hi", [P, DC, T], F32R)
        h_lo = sb("h_lo", [P, DC, T], F32R)
        hid_hi = sb("hid_hi", [P, FA, T], F32R)
        hid_lo = sb("hid_lo", [P, FA, T], F32R)
        with nc.sbuf_tensor("keys", [P, HEADS, T], F32) as keys:
            pass
        hid2 = sb("hid2", [P, 2, FC - FA, T], F32R)
        q_all = sb("q_all", [P, DC, T])
        q_rope = sb("q_rope", [P, 4, T])
        v_tok = sb("v_tok", [P, 3, D])
        raw = [sb(f"raw{s}", [P, UNIT]) for s in range(RING)]
        w_hi = [sb(f"w_hi{s}", [P, UNIT], F32R) for s in range(RING)]
        w_lo = [sb(f"w_lo{s}", [P, UNIT], F32R) for s in range(RING)]
        cst = sb("cst", [P, N_CONST])
        scores = sb("scores", [P, 2, SW])
        probs = sb("probs", [P, 4, PW])
        probs_t = sb("probs_t", [P, 2, PTW])
        q_aug = sb("q_aug", [P, 2, T])
        v_pair = sb("v_pair", [P, 2, 3, P])
        stats = sb("stats", [P, 2, 3, 3])
        sink_exp = sb("sink_exp", [P, 2, 3])
        rinv = sb("rinv", [P, 2, 3])
        y = sb("y", [P, 4, T])
        gated = sb("gated", [P, T])
        squares = sb("squares", [P, 2, T])
        total = sb("total", [P, T])
        rstd = sb("rstd", [P, T])
        eps = sb("eps", [P, 3])
        scales = sb("scales", [P, 2])
        ps = ctx.enter_context(nc.psum_tensor("ps", [P, 8, 512], F32))

        def c(name, rows=P):
            a, b = CONST[name]
            return cst[0:rows, a:b]

        shift, total_sq, mean_sq, mean = (y[:, i, :] for i in range(4))
        probs_flat = probs[:].rearrange("p s w -> p (s w)")
        ident, ones = c("ident"), c("ones")
        ln_par = c("ln").rearrange("p (n two k) -> p n two k", two=2, k=DC)
        conv_par = c("conv").rearrange("p (l j w) -> p l j w", l=DEPTH, w=4)
        gate_w = c("gate_w").rearrange("p (n k m) -> p n k m", n=2, k=DC)
        x_view = x.rearrange("k p t -> p k t")

        raw_landed = [sem(f"raw_landed{s}") for s in range(RING)]
        x_landed = [sem(f"x_landed{n}") for n in range(X_PARTS)]
        const_landed, out_stored = sem("const_landed"), sem("out_stored")
        hi_ready, lo_ready, w_used = sem("hi_ready"), sem("lo_ready"), sem("w_used")
        panel_done, bank_free = sem("panel_done"), sem("bank_free")
        init_done = sem("init_done")
        shift_sum, shift_ready, shifted = sem("shift_sum"), sem("shift_ready"), sem("shifted")
        mean_done, mean_squared, mean_copied = sem("mean_done"), sem("mean_squared"), sem("mean_copied")
        sq_mean_done, var_done, std_done = sem("sq_mean_done"), sem("var_done"), sem("std_done")
        total_added, sq_added, centered = sem("total_added"), sem("sq_added"), sem("centered")
        squared, rescaled, norm_hi = sem("squared"), sem("rescaled"), sem("norm_hi")
        affine_done, h_ready, out_ready = sem("affine_done"), sem("h_ready"), sem("out_ready")
        staged, scored, masked, negated = sem("staged"), sem("scored"), sem("masked"), sem("negated")
        exped, normed, transposed = sem("exped"), sem("normed"), sem("transposed")
        pt_copied, v_staged, mixed = sem("pt_copied"), sem("v_staged"), sem("mixed")
        o_hi, o_split = sem("o_hi"), sem("o_split")
        v_turned, v_copied = sem("v_turned"), sem("v_copied")
        ones_row, decay_moved = sem("ones_row"), sem("decay_moved")
        gate_done, gate_act, decay_done = sem("gate_done"), sem("gate_act"), sem("decay_done")
        swapped, roped, rope_key = sem("swapped"), sem("roped"), sem("rope_key")
        lat_sq, lat_sum, lat_std, lat_scaled, lat_hi, lat_ready = (
            sem(n) for n in ("lat_sq", "lat_sum", "lat_std", "lat_scaled", "lat_hi", "lat_ready"))
        conv_begun, silu_done, gate_mul, hid_hi_done, hid_ready = (
            sem(n) for n in ("conv_begun", "silu_done", "gate_mul", "hid_hi_done", "hid_ready"))
        dve_own, act_own, pool_own = sem("dve_own"), sem("act_own"), sem("pool_own")

        class Own:

            def __init__(self, eng, s):
                self.eng, self.s, self.base, self.k = eng, s, 0, 0
                self.i, self.per, self.looping = 0, 0, False

            def turn(self, i, per, first=0):
                if not self.looping:
                    self.base += self.k
                self.i, self.per, self.k, self.looping = i, per, 0, True
                self.off = self.base - first * per

            def turned(self, turns):
                assert self.k == self.per, (self.k, self.per)
                self.base += turns * self.per
                self.k, self.looping = 0, False

            def link(self, ins):
                ins.then_inc(self.s, 1)
                self.k += 1
                value = self.i * self.per + (self.off + self.k) if self.looping else self.base + self.k
                self.eng.wait_ge(self.s, value)

        def bank(p):
            return ps[:, p % BANKS, 0:T]

        def at(buf, i):
            return buf[:, i, :] if isinstance(i, int) else \
                buf[:, bass.ds(i, 1), :].rearrange("p o t -> p (o t)")

        def v_t(m):
            return probs_flat[:, m * T:(m + 1) * T]

        def raw_lat(k):
            return probs_flat[:, k * T:(k + 1) * T]

        def hidden(part, k):
            k, least = k if isinstance(k, tuple) else (k, k)
            if least < FA:
                return at((hid_hi, hid_lo)[part], k)
            return at(hid2[:, part], k - FA)

        def turns(eng, n, emit, first=0):
            if n - first == 1:
                emit(first)
            elif n > first:
                with eng.Fori(first, n) as i:
                    emit(i)

        block = ctx.enter_context(nc.Block())

        @block.sync
        def _(sp):
            sp.dma_start(raw[0][:], weights[0]).then_inc(raw_landed[0], 16)
            for n in range(X_PARTS):
                part = slice(n * DC // X_PARTS, (n + 1) * DC // X_PARTS)
                sp.dma_start(h[:, part], x_view[:, part]).then_inc(x_landed[n], 16)
            for u in range(1, RING):
                sp.dma_start(raw[u][:], weights[u]).then_inc(raw_landed[u], 16)
            sp.dma_start(cst[:], consts).then_inc(const_landed, 16)

            def unit(u, s):
                sp.wait_ge(lo_ready, u - (RING - 1))
                src = weights[u] if isinstance(u, int) else weights[bass.ds(u, 1)].rearrange("a p n -> p (a n)")
                sp.dma_start(raw[s][:], src).then_inc(raw_landed[s], 16)

            full = N_UNITS // RING
            with sp.Fori(1, full) as i:
                for s in range(RING):
                    unit(i * RING + s, s)
            for u in range(full * RING, N_UNITS):
                unit(u, u % RING)

            for chunk in range(DC):
                sp.wait_ge(out_ready, chunk + 1)
                sp.dma_start(out[chunk], h[:, chunk, N_META:T]).then_inc(out_stored, 16)
            sp.wait_ge(out_stored, 16 * DC)

        @block.tensor
        def _(pe):
            def panel(s, u0, p0, i, j, rhs, ready, t0):
                pn = i * s.body + (p0 + j)
                b = bank(p0 + j)[:, t0:T]
                if not (isinstance(pn, int) and pn < BANKS):
                    pe.wait_ge(bank_free, pn - (BANKS - 1))
                tiles = s.panels[j]
                new = set(s.new_units(j))
                for n, (u, t, k) in enumerate(tiles):
                    un = i * s.body_units + (u0 + u)
                    first = u in new
                    if first:
                        pe.wait_ge(lo_ready, un + 1)
                        new.discard(u)
                    if ready is not None and j == 0 and isinstance(i, int) and i == 0:
                        ready(k)
                    slot = (u0 + u) % RING
                    whi, wlo = w_hi[slot][:, t * P:(t + 1) * P], w_lo[slot][:, t * P:(t + 1) * P]
                    xhi, xlo = (x_part[:, t0:T] for x_part in rhs(k))
                    m = pe.matmul(b, whi, xhi, start=n == 0, stop=False)
                    if first and not (isinstance(un, int) and un == 0):
                        m.then_inc(w_used, 1)
                    pe.matmul(b, whi, xlo, start=False, stop=False)
                    m = pe.matmul(b, wlo, xhi, start=False, stop=n == len(tiles) - 1)
                m.then_inc(panel_done, 1)

            def leading_panels(s, u0, p0, rhs, ready, count, t0):
                for k in range(DC):
                    ready(k)
                    for j in range(count):
                        b, slot = bank(p0 + j)[:, t0:T], (u0 + j) % RING
                        if k == 0:
                            if p0 + j >= BANKS:
                                pe.wait_ge(bank_free, p0 + j - (BANKS - 1))
                            pe.wait_ge(lo_ready, u0 + j + 1)
                        whi, wlo = w_hi[slot][:, k * P:(k + 1) * P], w_lo[slot][:, k * P:(k + 1) * P]
                        xhi, xlo = (x_part[:, t0:T] for x_part in rhs(k))
                        m = pe.matmul(b, whi, xhi, start=k == 0, stop=False)
                        if (k == 0 and j == 0 and u0) or (k == DC - 1 and j):
                            m.then_inc(w_used, 1)
                        pe.matmul(b, whi, xlo, start=False, stop=False)
                        m = pe.matmul(b, wlo, xhi, start=False, stop=k == DC - 1)
                        if k == DC - 1:
                            m.then_inc(panel_done, 1)

            def gemm(layer, name, rhs, ready=None, after=None, lead=0, straight=False):
                s, u0, p0 = LAYERS[layer][name]
                t0 = LAST_FROM.get(name, 0) if layer == DEPTH - 1 else 0

                def turn(i):
                    for j in range(s.body):
                        if isinstance(i, int) and i == 0 and j < lead:
                            if j == 0:
                                leading_panels(s, u0, p0, rhs, ready, lead, t0)
                        else:
                            panel(s, u0, p0, i, j, rhs, ready, t0)
                        if after is not None:
                            after(i, j)

                if straight:
                    for i in range(s.turns):
                        turn(i)
                elif lead:
                    turn(0)
                    turns(pe, s.turns, turn, first=1)
                else:
                    turns(pe, s.turns, turn)

            def from_h(k):
                return h_hi[:, k, :], h_lo[:, k, :]

            def from_first(k):
                return hid_hi[:, k, :], hid_lo[:, k, :]

            def from_latent(first):
                return lambda k: (hid_hi[:, LAT + first + k, :], hid_lo[:, LAT + first + k, :])

            def from_hidden(k):
                return hidden(0, k), hidden(1, k)

            def norm_ready(n):
                return lambda k: pe.wait_ge(h_ready, 8 * n + k + 1)

            n_v = [0]

            def turn_value(m):
                b = ps[:, 4 + m % 2]
                if m >= 2:
                    pe.wait_ge(v_copied, n_v[0] + m - 1)
                for ch in (2, 0, 1):
                    a, e = ch * P, min(T, (ch + 1) * P)
                    t = pe.transpose(b[0:e - a, ch * P:(ch + 1) * P], v_t(m)[:, a:e], ident)
                t.then_inc(v_turned, 1)

            def attention(a, kind):
                rows = K_ROWS[kind]
                h0 = HEADS * a

                def step(i, j, scoring=True, turning=True, mixing=True):
                    hn = i * 4 + j
                    looping = not isinstance(hn, int)
                    if scoring:
                        s = j % 2
                        key = hn // 8 if kind == "swa" else hn
                        pe.wait_ge(staged, hn + (h0 + 1))
                        if looping or hn >= 4:
                            pe.wait_ge(masked, hn + (h0 - 3))
                        for ch, (lo, hi) in enumerate(CHUNKS):
                            hi_q = max(hi, P) if kind == "swa" else hi
                            m = pe.matmul(ps[0:hi_q - lo, j, SCOL[ch]:SCOL[ch + 1]], q_aug[0:rows, s, lo:hi_q],
                                          at(keys, key)[0:rows, 0:hi], start=True, stop=True)
                        m.then_inc(scored, 1)
                    if turning:
                        s = (j - 3) % 2
                        pe.wait_ge(normed, hn + (h0 - 2))
                        if looping or hn >= 4:
                            pe.wait_ge(pt_copied, hn + (h0 - 3))
                        b, pr = ps[:, 4 + s], probs[:, (j - 3) % 4]

                        def turn(col, ch, key, keys_n=P):
                            q = CHUNKS[ch][1] - CHUNKS[ch][0]
                            c0 = PCOL[ch] + key
                            return pe.transpose(b[0:keys_n, col:col + q], pr[0:q, c0:c0 + keys_n], ident[0:q, 0:q])

                        turn(PT1 + TAIL - P, 1, P)
                        turn(PTW - P, 2, 2 * P, TAIL)
                        turn(0, 0, 0)
                        turn(N_META, 1, 0)
                        turn(N_META + P, 2, 0)
                        turn(PT1 + TAIL, 2, P).then_inc(transposed, 1)
                    if mixing:
                        s = (j - 4) % 2
                        pe.wait_ge(pt_copied, hn + (h0 - 3))
                        pe.wait_ge(v_staged, hn + (h0 - 3))
                        o = ps[:, 6 + ((j - 4) // 2) % 2]
                        pt = probs_t[:, s]
                        pe.matmul(o[:, 0:T], v_pair[:, s, 0], pt[:, 0:T], start=s == 0, stop=False)
                        pe.matmul(o[:, P:T], v_pair[:, s, 1], pt[:, PT1:PT2], start=False, stop=False)
                        pe.matmul(o[:, 2 * P:T], v_pair[0:TAIL, s, 2], pt[0:TAIL, PT2:PTW], start=False,
                                  stop=s == 1).then_inc(mixed, 1)

                for j in range(4):
                    step(0, j, turning=j >= 3, mixing=False)
                with pe.Fori(1, 4) as i:
                    for j in range(4):
                        step(i, j)
                for j in range(4):
                    step(4, j, scoring=False, turning=j < 3)

            def output(n, stage, rhs, ready=None):
                p0 = LAYERS[n // 2][stage][2]

                def after(i, j):
                    if (i, j) == (0, 1):
                        pe.wait_ge(bank_free, p0 + 1)
                        pe.matmul(ps[:, 5, 0:T], ones, h[:, 0, :], start=True, stop=True).then_inc(shift_sum, 1)

                gemm(n // 2, stage, rhs, ready, after, straight=True)
                pe.wait_ge(shift_ready, n + 1)
                pe.wait_ge(total_added, 6 * (n + 1))
                pe.matmul(ps[:, 5, 0:T], ones, total[:], start=True, stop=False)
                pe.wait_ge(sq_added, 6 * (n + 1))
                pe.matmul(ps[:, 6, 0:T], ones, total_sq, start=True, stop=False)
                pe.wait_ge(bank_free, p0 + 8)
                pe.matmul(ps[:, 5, 0:T], ones, h[:, 7, :], start=False, stop=True).then_inc(mean_done, 1)
                pe.wait_ge(squared, 8 * n + 8)
                pe.matmul(ps[:, 6, 0:T], ones, squares[:, 1, :], start=False, stop=True).then_inc(sq_mean_done, 1)
                if n < 2 * DEPTH - 1:
                    slot = LAYERS[(n + 1) // 2][NEXT[n]][1] % RING
                    pe.wait_ge(hi_ready, LAYERS[(n + 1) // 2][NEXT[n]][1] + 1)
                    with pe.Fori(0, WARM // 4):
                        for _ in range(4):
                            pe.matmul(ps[:, 7, 0:T], w_hi[slot][:, 0:P], w_hi[slot][:, P:P + T], start=True, stop=True)

            n_swap = [0]
            n_fox = 0
            for a, kind in enumerate(KINDS):
                nr = norm_ready(2 * a)
                if kind == "fox":
                    gemm(a, "v", from_h, nr, lead=3 if a else 1)
                    if a == 0:
                        pe.wait_ge(const_landed, 16)
                    pe.wait_ge(bank_free, LAYERS[a]["q"][2])
                    gemm(a, "q", from_h, after=lambda i, j: turn_value(i * 4 + j), straight=True)
                    n_v[0] += 8
                    if a:
                        pe.wait_ge(affine_done, 8 * 2 * a)
                    for k in range(DC):
                        m = pe.matmul(ps[0:16, 6, 0:T], gate_w[:, n_fox, k, :], h[:, k, :],
                                      start=k == 0, stop=k == DC - 1)
                    m.then_inc(gate_done, 1)
                    gemm(a, "k", from_h)
                    pe.wait_ge(decay_moved, 16 * (n_fox + 1))
                    pe.wait_ge(ones_row, n_fox + 1)
                    n_fox += 1
                elif kind == "swa":
                    perm = c("perm_swa")
                    gemm(a, "vk", from_h, nr, lead=2)

                    def swap(src, done):
                        pe.wait_ge(bank_free, done)
                        pe.wait_ge(roped, n_swap[0])
                        pe.matmul(ps[:, 7, 0:T], perm, src, start=True, stop=True).then_inc(swapped, 1)
                        n_swap[0] += 1

                    swap(q_rope[:, 0, :], LAYERS[a]["vk"][2] + 2)
                    base = n_swap[0]
                    pq = LAYERS[a]["q"][2]

                    def swap_q(i, j):
                        pe.wait_ge(bank_free, i * 4 + (pq + j))
                        pe.wait_ge(roped, i * 4 + (base + j - 1))
                        pe.matmul(ps[:, 7, 0:T], perm, at(q_all, i * 4 + (j - 1)),
                                  start=True, stop=True).then_inc(swapped, 1)

                    def after(i, j):
                        if i or j:
                            swap_q(i, j)
                        else:
                            turn_value(0)

                    gemm(a, "q", from_h, after=after, straight=True)
                    swap_q(1, 4)
                    n_v[0] += 1
                    n_swap[0] += 8
                else:
                    perm = c("perm_mla")

                    def sum_squares(ks):
                        for k in ks:
                            pe.wait_ge(lat_sq, k + 1)
                            pe.matmul(ps[:, 5 if k < 3 else 6, 0:T], ones, y[:, k % 4, :],
                                      start=k in (0, 3), stop=k in (2, 4)).then_inc(lat_sum, 1)

                    def after_a(i, j):
                        if j == 3:
                            sum_squares(range(3))

                    def after_q(i, j):
                        if j == 0:
                            sum_squares((3, 4))
                        if j == 1:
                            pe.wait_ge(roped, n_swap[0])
                            pe.matmul(ps[:, 7, 0:T], perm, raw_lat(5), start=True, stop=True).then_inc(swapped, 1)

                    gemm(a, "a", from_h, nr, after=after_a, lead=3)
                    gemm(a, "q", from_latent(0), lambda k: pe.wait_ge(lat_ready, k + 1), after=after_q,
                         straight=True)
                    n_swap[0] += 1
                    pr = LAYERS[a]["r"][2]
                    base = n_swap[0]

                    def swap_r(j):
                        pe.wait_ge(bank_free, pr + j + 1)
                        pe.wait_ge(roped, base + j)
                        pe.matmul(ps[:, 7, 0:T], perm, q_rope[:, j, :], start=True, stop=True).then_inc(swapped, 1)

                    def after(i, j):
                        if j:
                            swap_r(j - 1)

                    gemm(a, "r", from_latent(0), after=after)
                    swap_r(3)
                    n_swap[0] += 4
                    pe.wait_ge(lat_ready, 5)
                    gemm(a, "v", from_latent(3))
                    pe.wait_ge(bank_free, LAYERS[a]["k"][2])
                    gemm(a, "k", from_latent(3), after=lambda i, j: turn_value(j))
                    n_v[0] += 8
                pe.wait_ge(v_copied, n_v[0])
                pe.wait_ge(bank_free, LAYERS[a]["o"][2])
                if ROPES[a]:
                    pe.wait_ge(roped, ROPES[a])
                if kind == "mla":
                    pe.wait_ge(rope_key, 1)
                attention(a, kind)
                pe.wait_ge(o_split, 8 * (a + 1))
                output(2 * a, "o", from_first)
                gemm(a, "up", from_h, norm_ready(2 * a + 1), lead=3)
                output(2 * a + 1, "down", from_hidden, lambda k: pe.wait_ge(hid_ready, FC * a + k + 1))

        @block.scalar
        def _(act):
            own = Own(act, act_own)

            def split_hi(u):
                u, slot, rounds = u
                act.wait_ge(raw_landed[slot], rounds * 16)
                if not (isinstance(u, int) and u < RING):
                    act.wait_ge(w_used, u - (RING - 1))
                act.activation(w_hi[slot][:], raw[slot][:], ACT.Copy).then_inc(hi_ready, 1)

            def units_of(layer, name, i, j):
                s, u0, _ = LAYERS[layer][name]
                for u in s.new_units(j):
                    first = u0 + u + AHEAD
                    if isinstance(i, int) and i * s.body_units + first >= N_UNITS:
                        continue
                    yield (i * s.body_units + first, first % RING,
                           i * (s.body_units // RING) + (first // RING + 1)
                           if s.turns > 1 else first // RING + 1)

            def gemm(layer, name, evac=None, links=0, straight=False):
                s, _, p0 = LAYERS[layer][name]

                def turn(i):
                    own.turn(i, links)
                    for j in range(s.body):
                        for u in units_of(layer, name, i, j):
                            split_hi(u)
                        if evac is not None:
                            evac(i, j, i * s.body + (p0 + j))

                if straight:
                    for i in range(s.turns):
                        turn(i)
                else:
                    turns(act, s.turns, turn)
                own.turned(s.turns)

            n_v = [0]

            def copy_value(m):
                act.wait_ge(v_turned, n_v[0] + m + 1)
                b = ps[:, 4 + m % 2]
                act.activation(v_tok[0:16, 2, m * P:(m + 1) * P], b[0:16, 2 * P:3 * P], ACT.Copy)
                act.activation(v_tok[:, 0:2, m * P:(m + 1) * P],
                               b[:, 0:2 * P].rearrange("p (c n) -> p c n", c=2), ACT.Copy).then_inc(v_copied, 1)

            def attention(a, kind):
                h0 = HEADS * a

                def step(i, j, exping=True, copying=True, outputs=True):
                    hn = i * 4 + j
                    looping = not isinstance(hn, int)
                    if copying:
                        s = (j - 3) % 2
                        act.wait_ge(transposed, hn + (h0 - 2))
                        if looping or hn >= 5:
                            act.wait_ge(mixed, hn + (h0 - 4))
                        act.activation(probs_t[:, s, 0:PT2], ps[:, 4 + s, 0:PT2], ACT.Copy)
                        act.activation(probs_t[0:TAIL, s, PT2:PTW], ps[0:TAIL, 4 + s, PT2:PTW],
                                       ACT.Copy).then_inc(pt_copied, 1)
                    if exping:
                        s = j % 2
                        act.wait_ge(negated, hn + (h0 + 1))
                        if looping or hn >= 4:
                            act.wait_ge(transposed, hn + (h0 - 3))
                        if kind == "swa":
                            a0, _ = CONST["sinks"]
                            sk = cst[:, a0 + hn:a0 + hn + 1] if isinstance(hn, int) else cst[:, bass.ds(hn + a0, 1)]
                            act.activation(sink_exp[:, s, :], stats[:, s, 1, :], ACT.Exp, bias=sk)
                        for ch, (lo, hi) in enumerate(CHUNKS):
                            r = hi - lo
                            ins = act.activation(probs[0:r, j, PCOL[ch]:PCOL[ch] + hi],
                                                 scores[0:r, s, SCOL[ch]:SCOL[ch + 1]], ACT.Exp,
                                                 bias=stats[0:r, s, 1, ch:ch + 1],
                                                 accum_out=stats[0:r, s, 2, ch:ch + 1])
                        ins.then_inc(exped, 1)
                    if outputs and j % 2 == 1:
                        act.wait_ge(mixed, hn + (h0 - 3))
                        act.activation(at(hid_hi, i * 2 + (j - 5) // 2), ps[:, 6 + ((j - 5) // 2) % 2, 0:T],
                                       ACT.Copy).then_inc(o_hi, 1)

                for j in range(4):
                    step(0, j, copying=j >= 3, outputs=False)
                first = 1
                if a == 0:
                    for j in range(4):
                        step(1, j)
                    first = 2
                with act.Fori(first, 4) as i:
                    for j in range(4):
                        step(i, j)
                for j in range(4):
                    step(4, j, exping=False, copying=j < 3)

            def square(n, k):
                p0 = LAYERS[n // 2]["down" if n % 2 else "o"][2]
                act.wait_ge(bank_free, p0 + k + 1)
                if k == 0:
                    act.wait_ge(shifted, n + 1)
                if k >= 2:
                    act.wait_ge(sq_added, 6 * n + max(1, k - 2))
                elif n and k == 1:
                    act.wait_ge(sq_mean_done, n)
                act.activation(squares[:, k % 2, :], h[:, k, :], ACT.Square).then_inc(squared, 1)

            def output(n, stage):

                def after(i, j, pn):
                    k = i * 4 + j
                    if k == 1:
                        act.wait_ge(shift_sum, n + 1)
                        act.activation(shift, ps[:, 5, 0:T], ACT.Copy, scale=float(DC)).then_inc(shift_ready, 1)
                    if k == 2:
                        square(n, 0)
                    if k >= 2:
                        square(n, k - 1)

                gemm(n // 2, stage, after, straight=True)
                act.activation(eps[:, 2:3], eps[:, 0:1], ACT.Sqrt)
                square(n, 7)
                act.wait_ge(mean_done, n + 1)
                act.activation(mean, ps[:, 5, 0:T], ACT.Copy).then_inc(mean_copied, 1)
                act.wait_ge(mean_copied, n + 1)
                act.activation(mean_sq, mean, ACT.Square).then_inc(mean_squared, 1)
                act.wait_ge(var_done, n + 1)
                act.activation(rstd[:], rstd[:], ACT.Sqrt, bias=eps[:, 0:1]).then_inc(std_done, 1)
                last = n == 2 * DEPTH - 1
                for k in range(DC):
                    act.wait_ge(rescaled, 8 * n + k + 1)
                    beta = ln_par[:, n, 1, k:k + 1]
                    if last:
                        act.activation(h[:, k, :], h[:, k, :], ACT.Identity, bias=beta).then_inc(out_ready, 1)
                    else:
                        act.activation(h_hi[:, k, :], h[:, k, :], ACT.Identity, bias=beta).then_inc(norm_hi, 1)

            split_hi((0, 0, 1))
            for k in range(DC):
                if k % (DC // X_PARTS) == 0:
                    act.wait_ge(x_landed[k * X_PARTS // DC], 16)
                act.activation(h_hi[:, k, :], h[:, k, :], ACT.Copy).then_inc(norm_hi, 1)
            for u in range(1, AHEAD):
                split_hi((u, u, 1))
            n_fox = 0
            for a, kind in enumerate(KINDS):
                if kind == "fox":
                    gemm(a, "v")
                    if a == 0:
                        act.wait_ge(const_landed, 16)
                        act.wait_ge(init_done, 7)
                    gemm(a, "q", lambda i, j, pn: copy_value(i * 4 + j), straight=True)
                    n_v[0] += 8
                    z, mag, e, u1, lnu = (y[0:16, 0, :], y[0:16, 1, :], y[0:16, 2, :], y[0:16, 3, :], gated[0:16, :])
                    act.wait_ge(gate_done, n_fox + 1)
                    gb = CONST["gate_b"][0] + n_fox
                    bias = cst[0:16, gb:gb + 1]
                    act.activation(z, ps[0:16, 6, 0:T], ACT.Identity, bias=bias)
                    own.link(act.activation(mag, ps[0:16, 6, 0:T], ACT.Abs, bias=bias))
                    own.link(act.activation(e, mag, ACT.Exp, scale=-1.0))
                    own.link(act.activation(u1, e, ACT.Identity, bias=1.0))
                    act.activation(lnu, u1, ACT.Ln).then_inc(gate_act, 1)
                    gemm(a, "k")
                    n_fox += 1
                elif kind == "swa":
                    gemm(a, "vk")
                    gemm(a, "q", lambda i, j, pn: copy_value(0) if i == j == 0 else None, straight=True)
                    n_v[0] += 1
                else:
                    pa = LAYERS[a]["a"][2]
                    g0 = CONST["rms_g"][0]

                    def square_latent(k):
                        act.wait_ge(bank_free, pa + k + 1)
                        if k >= 4:
                            act.wait_ge(lat_sum, k - 3)
                        act.activation(y[:, k % 4, :], raw_lat(k), ACT.Square).then_inc(lat_sq, 1)

                    def latent_root(n):
                        act.wait_ge(lat_sum, (3, 5)[n])
                        act.activation(squares[:, n, :], ps[:, 5 + n, 0:T], ACT.Sqrt,
                                       scale=float(D) / (Q_LORA, KV_LORA)[n], bias=eps[:, 1:2]).then_inc(lat_std, 1)

                    def latent_hi(k):
                        act.wait_ge(lat_scaled, k + 1)
                        act.activation(hid_hi[:, LAT + k, :], raw_lat(k), ACT.Identity,
                                       scale=cst[:, g0 + k:g0 + k + 1]).then_inc(lat_hi, 1)

                    def after_a(i, j, pn):
                        if j:
                            square_latent(j - 1)
                        if j == 4:
                            latent_root(0)

                    def after_q(i, j, pn):
                        if j == 0:
                            latent_root(1)
                        if j == 3:
                            latent_hi(3)
                            latent_hi(4)

                    gemm(a, "a", after_a)
                    for k in range(3):
                        latent_hi(k)
                    gemm(a, "q", after_q)
                    gemm(a, "r")
                    gemm(a, "v")
                    gemm(a, "k", lambda i, j, pn: copy_value(j))
                    n_v[0] += 8
                attention(a, kind)
                output(2 * a, "o")

                pu = LAYERS[a]["up"][2]

                def silu(k, slot):
                    act.wait_ge(bank_free, k * 2 + (pu + 1 - 2 * FC * a))
                    act.activation(y[:, 2 * slot, :], y[:, 2 * slot, :], ACT.Silu).then_inc(silu_done, 1)

                def hidden_hi(k, dst):
                    act.wait_ge(gate_mul, k + 1)
                    act.activation(dst, gated[:], ACT.Copy).then_inc(hid_hi_done, 1)

                def up_turn(least):
                    def turn(i):
                        for j in range(4):
                            if least or j >= 2:
                                k = i * 2 + (FC * a + j // 2 - 1)
                                if j % 2 == 0:
                                    silu(k, (j // 2 + 1) % 2)
                                else:
                                    hidden_hi(k, hidden(0, (i * 2 + (j // 2 - 1), least + j // 2 - 1)))
                            for u in units_of(a, "up", i, j):
                                split_hi(u)
                            idx = i * 4 + j
                            par = conv_par[:, a]
                            col = (lambda w: par[:, idx, w:w + 1]) if isinstance(idx, int) else \
                                (lambda w: par[:, bass.ds(idx, 1), w])
                            act.wait_ge(panel_done, i * 4 + (pu + j + 1))
                            act.activation(y[:, j, :], bank(pu + j), ACT.Identity,
                                           scale=col(2), bias=col(3)).then_inc(conv_begun, 1)
                    return turn

                turns(act, 1, up_turn(0))
                turns(act, SPLIT, up_turn(2), first=1)
                turns(act, FC // 2, up_turn(2 * SPLIT), first=SPLIT)
                silu(FC * a + FC - 1, 1)
                hidden_hi(FC * a + FC - 1, hidden(0, FC - 1))
                output(2 * a + 1, "down")

        @block.gpsimd
        def _(pool):
            own = Own(pool, pool_own)
            pool.memset(eps[:, 0:1], LN_EPS).then_inc(init_done, 1)
            pool.memset(eps[:, 1:2], RMS_EPS).then_inc(init_done, 1)
            pool.memset(scales[:, 0:1], SCALE["fox"]).then_inc(init_done, 1)
            pool.memset(scales[:, 1:2], SCALE["mla"]).then_inc(init_done, 1)
            for buf, value in ((stats, 1.0), (v_tok, 0.0), (v_pair, 0.0)):
                pool.memset(buf[:], value).then_inc(init_done, 1)

            def norm(n, stage):
                _, _, p0 = LAYERS[n // 2][stage]
                for k in range(1, DC - 1):
                    pool.wait_ge(bank_free, p0 + k + 1)
                    if k == 1:
                        pool.wait_ge(shifted, n + 1)
                        if n:
                            pool.wait_ge(sq_mean_done, n)
                    else:
                        pool.wait_ge(total_added, 6 * n + k - 1)
                    pool.tensor_tensor(total[:], h[:, 0, :] if k == 1 else total[:], h[:, k, :],
                                       ALU.add).then_inc(total_added, 1)
                    pool.wait_ge(squared, 8 * n + k + 1)
                    if k > 1:
                        pool.wait_ge(sq_added, 6 * n + k - 1)
                    pool.tensor_tensor(total_sq, squares[:, 0, :] if k == 1 else total_sq, squares[:, k % 2, :],
                                       ALU.add).then_inc(sq_added, 1)
                pool.wait_ge(mean_copied, n + 1)
                pool.wait_ge(squared, 8 * n + 8)
                for k in range(CENTER_DVE, DC):
                    pool.tensor_tensor(h[:, k, :], h[:, k, :], mean, ALU.subtract).then_inc(centered, 1)
                if n < 2 * DEPTH - 1:
                    for k in range(DC):
                        pool.wait_ge(h_ready, 8 * (n + 1) + k + 1)
                        pool.tensor_scalar(h[:, k, :], h[:, k, :], ln_par[:, n, 1, k:k + 1], None,
                                           ALU.add).then_inc(affine_done, 1)

            def attention(a, kind, n_v):
                h0 = HEADS * a
                n = 1 if kind == "mla" else 0
                scale = scales[:, n:n + 1].broadcast_to([P, T])

                def step(i, j, queries=True, values=True):
                    hn = i * 4 + j
                    looping = not isinstance(hn, int)
                    if queries:
                        s = j % 2
                        if looping or hn >= 2:
                            pool.wait_ge(scored, hn + (h0 - 1))
                        if looping or hn >= 5:
                            pool.wait_ge(v_staged, hn + (h0 - 4))
                        r = 64 * (j % 2)
                        src = at(q_all, i * 2 + j // 2)[r:r + 64]
                        ins = pool.tensor_tensor(q_aug[0:64, s, :], src, scale[r:r + 64], ALU.mult)
                        if kind == "mla":
                            src = at(q_rope, i)[32 * j:32 * j + 32]
                            own.link(ins)
                            ins = pool.tensor_tensor(q_aug[64:96, s, :], src, scale[32 * j:32 * j + 32], ALU.mult)
                        ins.then_inc(staged, 1)
                        pool.wait_ge(staged, hn + (h0 + 1))
                    if values:
                        s = j % 2
                        if looping or hn >= 6:
                            pool.wait_ge(mixed, hn + (h0 - 5))
                        col = ((hn - 4) // 8 if kind == "swa" else hn - 4) * HD
                        src = v_tok[:, :, col:col + HD] if isinstance(col, int) else v_tok[:, :, bass.ds(col, HD)]
                        pool.tensor_copy(v_pair[:, s, :, s * HD:(s + 1) * HD], src).then_inc(v_staged, 1)

                step(0, 0, values=False)
                step(0, 1, values=False)
                pool.wait_ge(v_copied, n_v)
                pool.memset(probs[:, :, N_META:P], 0.0)
                pool.memset(probs[:, :, PCOL[1] + CHUNKS[1][1]:PCOL[2]], 0.0)
                step(0, 2, values=False)
                step(0, 3, values=False)
                first = 1
                if a == 0:
                    for j in range(4):
                        step(1, j)
                    first = 2
                with pool.Fori(first, 4) as i:
                    own.turn(i, 4 if kind == "mla" else 0, first=first)
                    for j in range(4):
                        step(i, j)
                own.turned(4 - first)
                for j in range(4):
                    step(4, j, queries=False)

            n_fox = 0
            n_v = 0
            pool.wait_ge(init_done, 7)
            pool.wait_ge(const_landed, 16)
            for a, kind in enumerate(KINDS):
                n_v += 1 if kind == "swa" else DC
                if kind == "fox":
                    pool.wait_ge(decay_done, n_fox + 1)
                    pool.dma_start(keys[64:65, :, :], y[0:16, 1, :]).then_inc(decay_moved, 16)
                    n_fox += 1
                if kind != "swa":
                    pool.wait_ge(bank_free, LAYERS[a]["k" if kind == "fox" else "r"][2])
                if ROPES[a]:
                    pool.wait_ge(roped, ROPES[a])
                attention(a, kind, n_v)
                norm(2 * a, "o")
                pu = LAYERS[a]["up"][2]

                def gate(k, slot, hi, lo):
                    pool.wait_ge(bank_free, k * 2 + (pu + 2 - 2 * FC * a))
                    pool.wait_ge(silu_done, k + 1)
                    if not (isinstance(k, int) and k == 0):
                        pool.wait_ge(hid_ready, k)
                    pool.tensor_tensor(gated[:], y[:, 2 * slot, :], y[:, 2 * slot + 1, :],
                                       ALU.mult).then_inc(gate_mul, 1)
                    pool.wait_ge(hid_hi_done, k + 1)
                    pool.tensor_tensor(lo, gated[:], hi.bitcast(F32), ALU.subtract).then_inc(hid_ready, 1)

                def gate_turn(least):
                    def turn(i):
                        for n in range(2):
                            if least or n:
                                k = (i * 2 + (n - 1), least + n - 1)
                                gate(i * 2 + (FC * a + n - 1), (n + 1) % 2, hidden(0, k), hidden(1, k))
                    return turn

                turns(pool, 1, gate_turn(0))
                turns(pool, SPLIT, gate_turn(2), first=1)
                turns(pool, FC // 2, gate_turn(2 * SPLIT), first=SPLIT)
                gate(FC * a + FC - 1, 1, hidden(0, FC - 1), hidden(1, FC - 1))
                norm(2 * a + 1, "down")

        @block.vector
        def _(dve):
            own = Own(dve, dve_own)
            copy = dve.tensor_copy

            def tt(out_, a_, b_, op):
                return dve.tensor_tensor(out_, a_, b_, op)

            def split_lo(u, slot):
                dve.wait_ge(hi_ready, u + 1)
                tt(w_lo[slot][:], raw[slot][:], w_hi[slot][:].bitcast(F32), ALU.subtract).then_inc(lo_ready, 1)

            def split_units(layer, name, i, j):
                s, u0, _ = LAYERS[layer][name]
                for u in s.new_units(j):
                    first = u0 + u + AHEAD
                    if isinstance(i, int) and i * s.body_units + first >= N_UNITS:
                        continue
                    split_lo(i * s.body_units + first, first % RING)

            def gemm(layer, name, evac, links=0, before=None, straight=False):
                s, _, p0 = LAYERS[layer][name]

                def turn(i):
                    if links is not None:
                        own.turn(i, links)
                    for j in range(s.body):
                        split_units(layer, name, i, j)
                        if before is not None:
                            before(i, j)
                        dve.wait_ge(panel_done, i * s.body + (p0 + j + 1))
                        evac(i, j, bank(p0 + j), i * s.body + (p0 + j))

                if straight:
                    for i in range(s.turns):
                        turn(i)
                else:
                    turns(dve, s.turns, turn)
                if links is not None:
                    own.turned(s.turns)

            def to_q(body):
                def evac(i, j, b, pn):
                    copy(at(q_all, i * body + j), b).then_inc(bank_free, 1)
                return evac

            def to_v_t(body):
                def evac(i, j, b, pn):
                    m = i * body + j
                    dst = v_t(m) if isinstance(m, int) else probs_flat[:, bass.ds(m * T, T)]
                    copy(dst, b).then_inc(bank_free, 1)
                return evac

            def to_keys(body):
                def evac(i, j, b, pn):
                    m2 = i * (2 * body) + 2 * j
                    copy(keys_at(m2), b[0:64])
                    copy(keys_at(m2 + 1), b[64:128]).then_inc(bank_free, 1)
                return evac

            def keys_at(n):
                return at(keys, n)[0:64]

            def rope(qn, swap_no, cos, sin, dst, rows=P):
                tt(y[0:rows, 0, :], qn[0:rows], cos[0:rows], ALU.mult)
                dve.wait_ge(swapped, swap_no)
                own.link(tt(y[0:rows, 1, :], ps[0:rows, 7, 0:T], sin[0:rows], ALU.mult))
                return tt(dst, y[0:rows, 0, :], y[0:rows, 1, :], ALU.add)

            def attention(a, kind):
                h0, p0 = HEADS * a, HEADS // 2 * a
                mask = c("mask_window" if kind == "swa" else "mask_causal")

                def step(i, j, masking=True, norming=True, splitting=True):
                    hn = i * 4 + j
                    if masking:
                        s = j % 2
                        dve.wait_ge(scored, hn + (h0 + 1))
                        dve.memset(stats[:, s, 2, :], 1.0)
                        for ch, (lo, hi) in enumerate(CHUNKS):
                            r, cols = hi - lo, slice(SCOL[ch], SCOL[ch + 1])
                            ins = dve.tensor_tensor_reduce(
                                out=scores[0:r, s, cols], in0=ps[0:r, j, cols],
                                in1=mask[0:r, cols], scale=1.0, scalar=-3.0e38, op0=ALU.add, op1=ALU.max,
                                accum_out=stats[0:r, s, 0, ch:ch + 1])
                        ins.then_inc(masked, 1)
                        dve.wait_ge(masked, hn + (h0 + 1))
                        if kind == "swa":
                            a0, _ = CONST["sinks"]
                            sk = cst[:, a0 + hn:a0 + hn + 1] if isinstance(hn, int) else cst[:, bass.ds(hn + a0, 1)]
                            dve.tensor_scalar(stats[:, s, 1, :], stats[:, s, 0, :], sk, -1.0,
                                              ALU.max, ALU.mult).then_inc(negated, 1)
                        else:
                            dve.tensor_scalar(stats[:, s, 1, :], stats[:, s, 0, :], -1.0, None,
                                              ALU.mult).then_inc(negated, 1)
                    if norming:
                        s = (j - 1) % 2
                        dve.wait_ge(exped, hn + h0)
                        if kind == "swa":
                            own.link(tt(stats[:, s, 2, :], stats[:, s, 2, :], sink_exp[:, s, :], ALU.add))
                        own.link(dve.reciprocal(rinv[:, s, :], stats[:, s, 2, :]))
                        for ch, (lo, hi) in enumerate(CHUNKS):
                            pr = probs[0:hi - lo, (j - 1) % 4, PCOL[ch]:PCOL[ch] + hi]
                            ins = dve.tensor_scalar(pr, pr, rinv[0:hi - lo, s, ch:ch + 1], None, ALU.mult)
                        ins.then_inc(normed, 1)
                    if splitting and j % 2 == 1:
                        pair = i * 2 + (j - 5) // 2
                        dve.wait_ge(o_hi, pair + (p0 + 1))
                        tt(at(hid_lo, pair), ps[:, 6 + ((j - 5) // 2) % 2, 0:T],
                           at(hid_hi, pair).bitcast(F32), ALU.subtract).then_inc(o_split, 1)

                for j in range(4):
                    step(0, j, norming=j >= 1, splitting=False)
                with dve.Fori(1, 4) as i:
                    own.turn(i, 8 if kind == "swa" else 4, first=1)
                    for j in range(4):
                        step(i, j)
                own.turned(3)
                for j in range(4):
                    step(4, j, masking=False, norming=j < 1)

            def output(n, stage):

                def before(i, j):
                    k = i * 4 + j
                    if k == 0 and n:
                        dve.wait_ge(affine_done, 8 * n)
                    if k == 1:
                        dve.wait_ge(shift_ready, n + 1)
                        tt(h[:, 0, :], h[:, 0, :], shift, ALU.subtract).then_inc(shifted, 1)
                    if k:
                        own.link(dve.scalar_tensor_tensor(h[:, k, :], h[:, k, :], ALPHA, shift,
                                                          ALU.mult, ALU.subtract))

                def join(i, j, b, pn):
                    k = i * 4 + j
                    if k:
                        tt(h[:, k, :], h[:, k, :], b, ALU.add).then_inc(bank_free, 1)
                    else:
                        dve.scalar_tensor_tensor(h[:, 0, :], h[:, 0, :], ALPHA, b,
                                                 ALU.mult, ALU.add).then_inc(bank_free, 1)

                gemm(n // 2, stage, join, links=None, before=before, straight=True)

                last = n == 2 * DEPTH - 1
                dve.wait_ge(mean_copied, n + 1)
                dve.wait_ge(squared, 8 * n + CENTER_DVE)
                for k in range(CENTER_DVE):
                    tt(h[:, k, :], h[:, k, :], mean, ALU.subtract)
                    if k == 1:
                        dve.wait_ge(mean_squared, n + 1)
                        dve.wait_ge(sq_mean_done, n + 1)
                        tt(rstd[:], ps[:, 6, 0:T], mean_sq, ALU.subtract).then_inc(var_done, 1)
                dve.wait_ge(std_done, n + 1)
                own.link(dve.reciprocal(rstd[:], rstd[:]))

                def lo_part(k):
                    dve.wait_ge(norm_hi, 8 * (n + 1) + k + 1)
                    dve.scalar_tensor_tensor(h_lo[:, k, :], h[:, k, :], ln_par[:, n, 1, k:k + 1],
                                             h_hi[:, k, :].bitcast(F32), ALU.add, ALU.subtract).then_inc(h_ready, 1)

                for k in range(DC):
                    if k >= CENTER_DVE:
                        dve.wait_ge(centered, (DC - CENTER_DVE) * n + k - CENTER_DVE + 1)
                    dve.scalar_tensor_tensor(h[:, k, :], h[:, k, :], ln_par[:, n, 0, k:k + 1], rstd[:],
                                             ALU.mult, ALU.mult).then_inc(rescaled, 1)
                    if k and not last:
                        lo_part(k - 1)
                if not last:
                    lo_part(DC - 1)

            split_lo(0, 0)
            for k in range(DC):
                dve.wait_ge(norm_hi, k + 1)
                tt(h_lo[:, k, :], h[:, k, :], h_hi[:, k, :].bitcast(F32), ALU.subtract).then_inc(h_ready, 1)
            for u in range(1, AHEAD):
                split_lo(u, u)
            n_fox, n_swap = 0, 0
            for a, kind in enumerate(KINDS):
                if kind == "fox":
                    if a:
                        dve.wait_ge(scored, HEADS * a)
                    dve.memset(q_aug[64:65, :, 0:T], 1.0).then_inc(ones_row, 1)
                    gemm(a, "v", to_v_t(4))
                    if a == 0:
                        dve.wait_ge(const_landed, 16)
                        dve.wait_ge(init_done, 7)
                    gemm(a, "q", to_q(4))
                    z, mag, e, u1, lnu = (y[0:16, 0, :], y[0:16, 1, :], y[0:16, 2, :], y[0:16, 3, :], gated[0:16, :])
                    zero = squares[0:16, 0, :]
                    dve.wait_ge(gate_act, n_fox + 1)
                    own.link(dve.tensor_scalar(u1, u1, -1.0, None, ALU.add))
                    own.link(dve.tensor_scalar(zero, u1, 0.0, None, ALU.is_equal))
                    tt(lnu, lnu, zero, ALU.add)
                    own.link(tt(u1, u1, zero, ALU.add))
                    own.link(dve.reciprocal(u1, u1))
                    own.link(tt(lnu, lnu, u1, ALU.mult))
                    own.link(tt(lnu, lnu, e, ALU.mult))
                    own.link(dve.tensor_scalar(z, z, -1.0, 0.0, ALU.mult, ALU.max))
                    own.link(tt(lnu, lnu, z, ALU.add))
                    own.link(dve.tensor_scalar(zero, zero, 0.0, 1.0, ALU.mult, ALU.add))
                    dve.tensor_tensor_scan(mag, zero, lnu, 0.0, ALU.mult, ALU.add).then_inc(decay_done, 1)
                    gemm(a, "k", to_keys(4))
                    n_fox += 1
                elif kind == "swa":
                    cos, sin = c("cos_swa"), c("sin_swa")

                    def vk_evac(i, j, b, pn):
                        copy(v_t(0) if j == 0 else q_rope[:, 0, :], b).then_inc(bank_free, 1)

                    gemm(a, "vk", vk_evac)
                    dve.wait_ge(bank_free, LAYERS[a]["vk"][2] + 2)
                    n_swap += 1
                    own.link(rope(q_rope[:, 0, :], n_swap, cos, sin, q_rope[:, 0, :]))
                    copy(keys[0:64, 0, :], q_rope[0:64, 0, :])
                    copy(keys[0:64, 1, :], q_rope[64:128, 0, :]).then_inc(roped, 1)
                    base = n_swap

                    def rope_q(m):
                        dve.wait_ge(roped, base + m)
                        qn = q_all[:, m, :]
                        rope(qn, base + m + 1, cos, sin, qn).then_inc(roped, 1)

                    def q_evac(i, j, b, pn):
                        m = i * 4 + j
                        copy(q_all[:, m, :], b).then_inc(bank_free, 1)
                        dve.wait_ge(bank_free, pn + 1)
                        if m:
                            rope_q(m - 1)

                    gemm(a, "q", q_evac, links=None, straight=True)
                    rope_q(7)
                    n_swap += 8
                else:
                    cos, sin = c("cos_mla"), c("sin_mla")
                    g0 = CONST["rms_g"][0]

                    def scale_latent(k):
                        tt(raw_lat(k), raw_lat(k), squares[:, k // 3, :], ALU.mult).then_inc(lat_scaled, 1)

                    def latent_lo(k):
                        dve.wait_ge(lat_hi, k + 1)
                        dve.scalar_tensor_tensor(hid_lo[:, LAT + k, :], raw_lat(k), cst[:, g0 + k:g0 + k + 1],
                                                 hid_hi[:, LAT + k, :].bitcast(F32), ALU.mult,
                                                 ALU.subtract).then_inc(lat_ready, 1)

                    def latent_rstd(n):
                        dve.wait_ge(lat_std, n + 1)
                        own.link(dve.reciprocal(squares[:, n, :], squares[:, n, :]))

                    def before_a(i, j):
                        if j == 5:
                            latent_rstd(0)

                    def before_q(i, j):
                        if j == 2:
                            latent_rstd(1)
                        if j == 3:
                            scale_latent(3)
                            scale_latent(4)
                        if j == 4:
                            latent_lo(3)
                            latent_lo(4)

                    gemm(a, "a", lambda i, j, b, pn: copy(raw_lat(j), b).then_inc(bank_free, 1),
                         links=None, before=before_a, straight=True)
                    dve.wait_ge(lat_sq, 3)
                    scale_latent(0)
                    scale_latent(1)
                    latent_lo(0)
                    scale_latent(2)
                    latent_lo(1)
                    latent_lo(2)
                    gemm(a, "q", to_q(8), links=None, before=before_q, straight=True)
                    n_swap += 1
                    own.link(tt(scores[0:32, 0, 0:T], raw_lat(5)[0:32], cos[0:32], ALU.mult))
                    dve.wait_ge(swapped, n_swap)
                    tt(scores[0:32, 1, 0:T], ps[0:32, 7, 0:T], sin[0:32], ALU.mult).then_inc(roped, 1)
                    dve.wait_ge(roped, n_swap)
                    own.link(tt(scores[0:32, 0, 0:T], scores[0:32, 0, 0:T], scores[0:32, 1, 0:T], ALU.add))
                    base = n_swap

                    def shared_key(i, j):
                        ins = copy(keys[64:96, 2 * j:2 * j + 2, :],
                                   scores[0:32, 0, 0:T].unsqueeze(1).broadcast_to([32, 2, T]))
                        if j == 7:
                            ins.then_inc(rope_key, 1)

                    def rope_r(m):
                        dve.wait_ge(roped, base + m)
                        qn = q_rope[:, m, :]
                        rope(qn, base + m + 1, cos, sin, qn).then_inc(roped, 1)

                    def r_evac(i, j, b, pn):
                        copy(q_rope[:, j, :], b).then_inc(bank_free, 1)
                        dve.wait_ge(bank_free, pn + 1)
                        if j:
                            rope_r(j - 1)

                    gemm(a, "r", r_evac, links=None)
                    rope_r(3)
                    n_swap += 4
                    gemm(a, "v", to_v_t(8), before=shared_key)
                    gemm(a, "k", to_keys(8))
                attention(a, kind)
                output(2 * a, "o")

                def conv(i, j, b, pn):
                    idx = i * 4 + j
                    par = conv_par[:, a]
                    col = (lambda w: par[:, idx, w:w + 1]) if isinstance(idx, int) else \
                        (lambda w: par[:, bass.ds(idx, 1), w])
                    yj = y[:, j, :]
                    dve.wait_ge(conv_begun, i * 4 + (2 * FC * a + j + 1))
                    own.link(dve.scalar_tensor_tensor(yj[:, 1:T], b[:, 0:T - 1], col(1), yj[:, 1:T],
                                                      ALU.mult, ALU.add))
                    dve.scalar_tensor_tensor(yj[:, 2:T], b[:, 0:T - 2], col(0), yj[:, 2:T],
                                             ALU.mult, ALU.add).then_inc(bank_free, 1)

                gemm(a, "up", conv, links=4)
                output(2 * a + 1, "down")



def panels(w):
    k, n = w.shape
    return w.reshape(k // P, P, n // P, P).transpose(2, 1, 0, 3)


def units(w, per_unit=1):
    a = panels(w)
    n, _, kt, _ = a.shape
    a = a.reshape(n // per_unit, per_unit, P, kt, P).transpose(0, 2, 1, 3, 4).reshape(n // per_unit, P, -1)
    full = np.zeros((a.shape[0], P, UNIT), a.dtype)
    full[:, :, :a.shape[2]] = a
    return full


def down_units(w):
    a = panels(w)
    full = np.zeros((DC, 3, P, UNIT), w.dtype)
    k = 0
    for u, n in enumerate(DOWN_TILES):
        full[:, u, :, :n * P] = a[:, :, k:k + n].reshape(DC, P, n * P)
        k += n
    return full.reshape(3 * DC, P, UNIT)


def layer_units(a, kind, inp):
    j = a // 3
    if kind == "fox":
        w = inp["fox_w_in"][j]
        mixer = [w[:, 2 * D:3 * D], w[:, :D], w[:, D:2 * D], inp["fox_w_o"][j]]
        mixer = [units(m) for m in mixer]
    elif kind == "swa":
        w = inp["swa_w_in"][j]
        kd = 2 * HD
        mixer = [units(m) for m in (w[:, D + kd:], w[:, D:D + kd], w[:, :D], inp["swa_w_o"][j])]
    else:
        wa = inp["mla_w_a"][j]
        wide = np.zeros((D, 6 * P), wa.dtype)
        wide[:, :wa.shape[1]] = wa
        uq = inp["mla_w_uq"][j].reshape(Q_LORA, HEADS, HD + MLA_ROPE)
        ukv = inp["mla_w_ukv"][j].reshape(KV_LORA, HEADS, 2 * HD)
        mixer = [units(wide), units(uq[:, :, :HD].reshape(Q_LORA, D), 2),
                 units(uq[:, :, HD:].reshape(Q_LORA, HEADS * MLA_ROPE), 2),
                 units(ukv[:, :, HD:].reshape(KV_LORA, D), 4),
                 units(ukv[:, :, :HD].reshape(KV_LORA, D), 4), units(inp["mla_w_o"][j])]
    up = units(inp["ffn_w_in"][a])
    up = np.stack([up[:FC], up[FC:]], 1).reshape(2 * FC, P, UNIT)
    return mixer + [up, down_units(inp["ffn_w_out"][a])]


def rope_tables(dim, theta, period):
    inv = (np.float32(theta) ** (-np.arange(0, dim, 2, dtype=np.float32) / np.float32(dim))).astype(np.float32)
    ang = np.arange(T, dtype=np.float32)[:, None] * inv[None, :]
    cos, sin = np.ones((P, T), np.float32), np.zeros((P, T), np.float32)
    perm = np.zeros((P, P), np.float32)
    half = dim // 2
    for p in range(P):
        d = p % period
        if d < dim:
            cos[p] = np.cos(ang[:, d % half])
            sin[p] = np.sin(ang[:, d % half]) * (-1 if d < half else 1)
            perm[p + half if d < half else p - half, p] = 1.0
    return cos, sin, perm


def masks():
    both = []
    for window in (T, WINDOW):
        m = np.full((P, SW), NEG, np.float32)
        for ch, (lo, hi) in enumerate(CHUNKS):
            q, k = np.arange(lo, hi)[:, None], np.arange(hi)[None, :]
            seen = (k <= q) & ((q - k < window) | (k < N_META))
            m[:hi - lo, SCOL[ch]:SCOL[ch + 1]] = np.where(seen, 0.0, NEG)
        both.append(m)
    return both


def const_block(inp):
    block = np.zeros((P, N_CONST), np.float32)

    def put(name, a, rows=P):
        lo, hi = CONST[name]
        block[:rows, lo:hi] = a.reshape(rows, hi - lo)

    put("ident", np.eye(P, dtype=np.float32))
    put("ones", np.full((P, P), 1.0 / D, np.float32))
    for name, args in (("swa", (ROPE_DIM, 500000.0, HD)), ("mla", (MLA_ROPE, 10000.0, MLA_ROPE))):
        cos, sin, perm = rope_tables(*args)
        put("cos_" + name, cos)
        put("sin_" + name, sin)
        put("perm_" + name, perm)
    causal, window = masks()
    put("mask_causal", causal)
    put("mask_window", window)
    ln = np.stack([np.stack([inp["ln1_g"], inp["ln1_b"]], 1), np.stack([inp["ln2_g"], inp["ln2_b"]], 1)], 1)
    put("ln", ln.reshape(DEPTH * 4, DC, P).transpose(2, 0, 1))
    cv = np.concatenate([inp["ffn_conv_w"], inp["ffn_conv_b"][:, None]], 1)
    put("conv", cv.reshape(DEPTH, 4, 2, FC, P).transpose(4, 0, 3, 2, 1))
    put("sinks", np.broadcast_to(inp["swa_sinks"][0], (P, HEADS)))
    put("gate_b", inp["fox_b_f"].T, HEADS)
    put("gate_w", inp["fox_w_in"][:, :, 3 * D:].reshape(2, DC, P, HEADS).transpose(2, 0, 1, 3))
    g = np.concatenate([inp["mla_g_q"][0], inp["mla_g_kv"][0]])
    put("rms_g", g.reshape(5, P).T)
    return block


def kernel(**inputs):
    import concourse.bacc as bacc
    from concourse.bass_utils import run_bass_kernel_spmd

    inp = {k: np.asarray(v) for k, v in inputs.items()}
    tokens = np.concatenate([inp["meta_tokens"], inp["x"][0]], 0)
    arrays = {
        "in_x": np.ascontiguousarray(tokens.T.reshape(DC, P, T)),
        "in_weights": np.concatenate([u for a, kind in enumerate(KINDS) for u in layer_units(a, kind, inp)], 0),
        "in_consts": const_block(inp),
    }
    assert arrays["in_weights"].shape[0] == N_UNITS
    nc = bacc.Bacc("TRN2", target_bir_lowering=False, num_devices=1)
    args = [nc.dram_tensor(n, a.shape, mybir.dt.from_np(a.dtype), kind="ExternalInput").ap()
            for n, a in arrays.items()]
    out = nc.dram_tensor("out_0", (DC, P, SEQ), F32, kind="ExternalOutput").ap()
    build_program(nc, *args, out)
    got = run_bass_kernel_spmd(nc, [arrays], core_ids=[0]).results[0]["out_0"]
    return np.ascontiguousarray(got.reshape(D, SEQ).T)[None]
```
